# Optimizing a Trainium2 kernel written in Bass

```python
import jax, jax.numpy as jnp
from jax import lax
import numpy as np

D_MODEL = 2048
BATCH = 1
SEQ = 256
DEPTH = 2

N_MIXERS = 2
HEAD_DIM = 128
N_ATTN_HEADS = 12
ATTN_WIDTH = N_ATTN_HEADS * HEAD_DIM
Q_LORA = 512
KV_LORA = 256
IDX_HEADS = 16
IDX_DIM = 64
TOPK_MAX = 256
Q_BLOCK = 128
POOL_WINDOWS = (2, 4, 8, 16)
N_POOL_GROUPS = len(POOL_WINDOWS)
POOL_WIDTH = 1536
POOL_GROUP = POOL_WIDTH // N_POOL_GROUPS
N_MEM = 256
N_MEM_HEADS = 4
MEM_WIDTH = N_MEM_HEADS * HEAD_DIM
MIX_WIDTH = ATTN_WIDTH + MEM_WIDTH
D_FF = -(-8 * D_MODEL // (3 * 256)) * 256
ATTN_SPLITS = (Q_LORA, KV_LORA, IDX_DIM, IDX_HEADS, MEM_WIDTH)
ATTN_IN = sum(ATTN_SPLITS)
POOL_IN = POOL_WIDTH + MEM_WIDTH
N_ATTN_LAYERS = (DEPTH + 1) // 2
N_POOL_LAYERS = DEPTH // 2
EPS = 1e-6

kernel_name = "dsa_pool_hybrid_trunk"

def rmsnorm(x, g):
    xf = x.astype(jnp.float32)
    y = xf * lax.rsqrt(jnp.mean(xf * xf, axis=-1, keepdims=True) + EPS)
    return (y * g.astype(jnp.float32)).astype(x.dtype)

def layernorm(x, g, b):
    xf = x.astype(jnp.float32)
    mu = jnp.mean(xf, axis=-1, keepdims=True)
    var = jnp.mean(jnp.square(xf - mu), axis=-1, keepdims=True)
    y = (xf - mu) * lax.rsqrt(var + EPS)
    return (y * g.astype(jnp.float32) + b.astype(jnp.float32)).astype(x.dtype)

def split_cols(a, sizes):
    offs = np.cumsum(sizes)[:-1].tolist()
    return jnp.split(a, offs, axis=-1)

def dsa_mixer(h, w_in, q_norm, kv_norm, w_uq, w_uk, w_uv, w_idx_uq, idx_k_norm, idx_k_bias):
    B, T, _ = h.shape
    c_q, c_kv, k_idx, w_idx, q_mem = split_cols(h @ w_in, ATTN_SPLITS)
    c_q = rmsnorm(c_q, q_norm)
    c_kv = rmsnorm(c_kv, kv_norm)
    k_idx = layernorm(k_idx, idx_k_norm, idx_k_bias)
    q = (c_q @ w_uq).reshape(B, T, N_ATTN_HEADS, HEAD_DIM)
    q_abs = jnp.einsum('bthd,hcd->bthc', q, w_uk)
    q_idx = (c_q @ w_idx_uq).reshape(B, T, IDX_HEADS, IDX_DIM)
    w_idx = w_idx * (IDX_HEADS ** -0.5 * IDX_DIM ** -0.5)
    k_top = min(TOPK_MAX, T // 4)
    n_blk = T // Q_BLOCK
    key_pos = jnp.arange(T)
    scale = HEAD_DIM ** -0.5

    def block(i):
        t0 = i * Q_BLOCK
        qi = lax.dynamic_slice_in_dim(q_idx, t0, Q_BLOCK, 1)
        wi = lax.dynamic_slice_in_dim(w_idx, t0, Q_BLOCK, 1)
        qa = lax.dynamic_slice_in_dim(q_abs, t0, Q_BLOCK, 1)
        qpos = t0 + jnp.arange(Q_BLOCK)
        s = jax.nn.relu(jnp.einsum('bqhd,bsd->bqhs', qi, k_idx))
        score = jnp.einsum('bqh,bqhs->bqs', wi, s).astype(jnp.float32)
        causal = key_pos[None, :] <= qpos[:, None]
        score = jnp.where(causal[None], score, -jnp.inf)
        _, sel = lax.top_k(score, k_top)
        valid = sel <= qpos[None, :, None]
        c_sel = jax.vmap(lambda c, ix: c[ix])(c_kv, sel)
        logits = jnp.einsum('bqhc,bqkc->bqhk', qa, c_sel).astype(jnp.float32) * scale
        logits = jnp.where(valid[:, :, None, :], logits, -jnp.inf)
        p = jax.nn.softmax(logits, axis=-1).astype(c_sel.dtype)
        return jnp.einsum('bqhk,bqkc->bqhc', p, c_sel)

    o_lat = lax.map(block, jnp.arange(n_blk))
    o_lat = o_lat.transpose(1, 0, 2, 3, 4).reshape(B, T, N_ATTN_HEADS, KV_LORA)
    o = jnp.einsum('bthc,hcd->bthd', o_lat, w_uv).reshape(B, T, ATTN_WIDTH)
    return o, q_mem

def pool_mixer(h, w_in, w_group, scale):
    B, T, _ = h.shape
    proj = h @ w_in
    u, q_mem = proj[..., :POOL_WIDTH], proj[..., POOL_WIDTH:]
    uf = u.astype(jnp.float32)
    cs = jnp.concatenate([jnp.zeros((B, 1, POOL_WIDTH), jnp.float32), jnp.cumsum(uf, axis=1)], axis=1)
    pos = jnp.arange(T)
    outs = []
    for g, w in enumerate(POOL_WINDOWS):
        sl = slice(g * POOL_GROUP, (g + 1) * POOL_GROUP)
        seg = cs[..., sl]
        start = jnp.maximum(pos + 1 - w, 0)
        total = jnp.take(seg, pos + 1, axis=1) - jnp.take(seg, start, axis=1)
        cnt = (pos + 1 - start).astype(jnp.float32)
        outs.append(total / cnt[None, :, None] - uf[..., sl])
    y = jnp.stack(outs, axis=2).astype(u.dtype)
    y = jnp.einsum('btgc,gcd->btgd', y, w_group).reshape(B, T, POOL_WIDTH) * scale
    return y, q_mem

def mem_attend(q_mem, mem_k, mem_v):
    B, T = q_mem.shape[:2]
    logits = jnp.einsum('bthd,bnhd->bhtn', q_mem, mem_k).astype(jnp.float32) * HEAD_DIM ** -0.5
    p = jax.nn.softmax(logits, axis=-1).astype(mem_v.dtype)
    return jnp.einsum('bhtn,bnhd->bthd', p, mem_v).reshape(B, T, MEM_WIDTH)

def setup_inputs(seed: int = 0) -> dict:
    key = jax.random.key(seed)
    ks = iter(jax.random.split(key, 32))

    def nrm(shape, fan_in):
        return jax.random.normal(next(ks), shape, jnp.float32) * fan_in ** -0.5

    def gain(shape):
        return 1.0 + 0.1 * jax.random.normal(next(ks), shape, jnp.float32)

    return {
        "x": jax.random.normal(next(ks), (BATCH, SEQ, D_MODEL), jnp.float32),
        "mem": jax.random.normal(next(ks), (BATCH, N_MEM, D_MODEL), jnp.float32),
        "mixer_norm": gain((DEPTH, D_MODEL)),
        "ffn_norm": gain((DEPTH, D_MODEL)),
        "final_norm": gain((D_MODEL,)),
        "mem_norm": gain((D_MODEL,)),
        "w_mem_kv": nrm((DEPTH, D_MODEL, 2 * MEM_WIDTH), D_MODEL),
        "w_out": nrm((DEPTH, MIX_WIDTH, D_MODEL), MIX_WIDTH),
        "w_gate": nrm((DEPTH, D_MODEL, D_FF), D_MODEL),
        "w_up": nrm((DEPTH, D_MODEL, D_FF), D_MODEL),
        "w_down": nrm((DEPTH, D_FF, D_MODEL), D_FF),
        "w_in_attn": nrm((N_ATTN_LAYERS, D_MODEL, ATTN_IN), D_MODEL),
        "q_norm": gain((N_ATTN_LAYERS, Q_LORA)),
        "kv_norm": gain((N_ATTN_LAYERS, KV_LORA)),
        "w_uq": nrm((N_ATTN_LAYERS, Q_LORA, ATTN_WIDTH), Q_LORA),
        "w_uk": nrm((N_ATTN_LAYERS, N_ATTN_HEADS, KV_LORA, HEAD_DIM), HEAD_DIM),
        "w_uv": nrm((N_ATTN_LAYERS, N_ATTN_HEADS, KV_LORA, HEAD_DIM), KV_LORA),
        "w_idx_uq": nrm((N_ATTN_LAYERS, Q_LORA, IDX_HEADS * IDX_DIM), Q_LORA),
        "idx_k_norm": gain((N_ATTN_LAYERS, IDX_DIM)),
        "idx_k_bias": 0.02 * jax.random.normal(next(ks), (N_ATTN_LAYERS, IDX_DIM), jnp.float32),
        "w_in_pool": nrm((N_POOL_LAYERS, D_MODEL, POOL_IN), D_MODEL),
        "w_pool_group": nrm((N_POOL_LAYERS, N_POOL_GROUPS, POOL_GROUP, POOL_GROUP), POOL_GROUP),
        "pool_scale": gain((N_POOL_LAYERS, POOL_WIDTH)),
    }

def reference(x, mem, mixer_norm, ffn_norm, final_norm, mem_norm, w_mem_kv, w_out, w_gate, w_up, w_down,
              w_in_attn, q_norm, kv_norm, w_uq, w_uk, w_uv, w_idx_uq, idx_k_norm, idx_k_bias,
              w_in_pool, w_pool_group, pool_scale):
    B, T, _ = x.shape
    mem_n = rmsnorm(mem, mem_norm)
    for i in range(DEPTH):
        h = rmsnorm(x, mixer_norm[i])
        j = i // N_MIXERS
        if i % N_MIXERS == 0:
            y, q_mem = dsa_mixer(h, w_in_attn[j], q_norm[j], kv_norm[j], w_uq[j], w_uk[j], w_uv[j],
                                 w_idx_uq[j], idx_k_norm[j], idx_k_bias[j])
        else:
            y, q_mem = pool_mixer(h, w_in_pool[j], w_pool_group[j], pool_scale[j])
        kv = mem_n @ w_mem_kv[i]
        mk = kv[..., :MEM_WIDTH].reshape(B, N_MEM, N_MEM_HEADS, HEAD_DIM)
        mv = kv[..., MEM_WIDTH:].reshape(B, N_MEM, N_MEM_HEADS, HEAD_DIM)
        m = mem_attend(q_mem.reshape(B, T, N_MEM_HEADS, HEAD_DIM), mk, mv)
        x = x + jnp.concatenate([y, m], axis=-1) @ w_out[i]
        h = rmsnorm(x, ffn_norm[i])
        x = x + (jax.nn.silu(h @ w_gate[i]) * (h @ w_up[i])) @ w_down[i]
    return rmsnorm(x, final_norm)


_drawn_inputs = setup_inputs


def setup_inputs(seed=0):
    import zlib

    import numpy as np

    out = dict(_drawn_inputs(seed))
    spreads = {}
    factors = {'mem_norm': 5.353, 'idx_k_bias': 3.301}
    for name, (base, spread) in spreads.items():
        noise = np.random.default_rng([zlib.crc32(name.encode()), seed]).standard_normal(out[name].shape)
        drawn = base * np.exp(spread * noise) if base else spread * noise
        out[name] = __import__('jax').numpy.asarray(drawn.astype(out[name].dtype))
    for name, factor in factors.items():
        out[name] = (out[name] * factor).astype(out[name].dtype)
    return out
```

```python
from contextlib import ExitStack

import concourse.bass as bass
from concourse import mybir

F32 = mybir.dt.float32
F32R = mybir.dt.float32r
ACT = mybir.ActivationFunctionType
ALU = mybir.AluOpType
AX = mybir.AxisListType

P = 128
NW = 512
RING = 4
AHEAD = 3
NBANK = 4
EPS = 1e-6
FILL_BEFORE = {0: 0, 1: 4, 3: 8, 5: 12}
MASKED = -1.0e30
NONCAUSAL = -1.0e38
TAKEN = -3.0e38
TAKEN_BELOW = -2.0e38


def trunk(nc, x, mem, mixer_norm, ffn_norm, final_norm, mem_norm, w_mem_kv, w_out, w_gate, w_up, w_down,
          w_in_attn, q_norm, kv_norm, w_uq, w_uk, w_uv, w_idx_uq, idx_k_norm, idx_k_bias,
          w_in_pool, w_pool_group, pool_scale, out):
    _, T, D = x.shape
    TT = T // P
    KD = D // P
    DFF = w_gate.shape[2]
    KF = DFF // P
    LAYERS = w_out.shape[0]
    NH, KVL, HD = w_uk.shape[1:]
    QL = q_norm.shape[1]
    KQ, KC = QL // P, KVL // P
    ID = idx_k_norm.shape[1]
    IH = w_idx_uq.shape[2] // ID
    MW = w_mem_kv.shape[2] // 2
    MH = MW // HD
    PW = pool_scale.shape[1]
    NG, PG = w_pool_group.shape[1], w_pool_group.shape[2]
    KG = PG // P
    TOPK = min(256, T // 4)
    ATTN_IN = w_in_attn.shape[2]
    C_KV, C_KI, C_WI, C_QM = QL, QL + KVL, QL + KVL + ID, QL + KVL + ID + IH
    SCALE = HD ** -0.5
    assert TT == 2 and HD == P and MW == NW and 2 * ID == P and T == 2 * P and LAYERS == 2
    FFN_IT = DFF // NW
    CT_D, CT_F, CT_Q = KD // 2, KF // 2, KQ // 2
    KPC = NW // P

    TILE, CHUNK = {}, {}
    LAST = []
    tiles = 0
    for name, chunks, per in (("mem0", 2, CT_D), ("mem1", 2, CT_D), ("in0", 3, CT_D), ("idx", 2, CT_Q), ("uq", 3, CT_Q),
                              ("out0", 4, CT_D), ("ffn0", 2 * FFN_IT, CT_D), ("down0", 4, CT_F), ("in1", 4, CT_D),
                              ("out1", 4, CT_D), ("ffn1", 2 * FFN_IT, CT_D), ("down1", 4, CT_F)):
        TILE[name], CHUNK[name] = tiles, len(LAST)
        for _ in range(chunks):
            tiles += per
            LAST.append(tiles - 1)
    TILES = tiles
    JOB, jobs = {}, 0
    for name, count in (("gains", 1), ("memT", KD), ("mk0", MH), ("mk1", MH), ("h0", KD), ("cq", KQ), ("ckv", KC),
                        ("kidx", 1), ("qmem0", MH), ("qidx0", KPC), ("qidx1", KPC), ("q0", KPC), ("score", IH),
                        ("q1", KPC), ("q2", KPC), ("v", TT * NH // 4), ("k", NH // 2), ("head0", 3 * (NH + MH)),
                        ("f0", KD), ("hid0", KPC * FFN_IT), ("h1", KD),
                        ("pool01", 2 * KPC), ("group0", KG), ("pool2", KPC), ("group123", 3 * KG),
                        ("qmem1", MH), ("head1", 3 * MH), ("f1", KD), ("hid1", KPC * FFN_IT)):
        JOB[name] = jobs
        jobs += count
    TR, count = {}, 0
    for name, number in (("memT", KD), ("h0", KD), ("cq", KQ), ("head0", NH + MH), ("f0", KD), ("hid0", KPC * FFN_IT),
                         ("h1", KD), ("group0", KG), ("group123", 3 * KG), ("head1", MH), ("f1", KD),
                         ("hid1", KPC * FFN_IT)):
        TR[name] = count
        count += number

    X_CHUNKS = {"out0": 0, "down0": 4, "out1": 8, "down1": 12}

    def heads(layer):
        return [(False, h) for h in range(MH)] + ([(True, h) for h in range(NH)] if layer == 0 else [])

    def head_jobs(layer):
        number, n = {}, len(heads(layer))
        at = JOB[f"head{layer}"]
        for s in range(n + 2):
            for what, lag in (("logits", 0), ("probs", 1), ("output", 2)):
                if 0 <= s - lag < n:
                    number[what, s - lag] = at
                    at += 1
        return number

    def kt_of(is_self, h):
        return h if is_self else NH + h

    with ExitStack() as ctx:
        def sb(name, shape, dt=F32):
            return ctx.enter_context(nc.sbuf_tensor(name, shape, dt))

        def sem(name):
            return ctx.enter_context(nc.semaphore(name))

        xres = sb("xres", [P, TT, D])
        raw = sb("raw", [P, RING, 2, NW])
        whi = sb("whi", [P, RING, 2, NW], F32R)
        wlo = sb("wlo", [P, RING, 2, NW], F32R)
        stage = sb("stage", [P, TT, NW])
        mk1T = sb("mk1T", [P, MH, T])
        mv1 = sb("mv1", [P, TT, MW])
        ident = sb("ident", [P, P])
        GROWS = dict(mix=0, ffn=LAYERS * KD, mem=2 * LAYERS * KD, q=(2 * LAYERS + 1) * KD)
        GROWS["kv"] = GROWS["q"] + KQ
        GROWS["pool"] = GROWS["kv"] + KC
        GROWS["ki"] = GROWS["pool"] + PW // P
        GROWS["kb"] = GROWS["ki"] + 1
        NGR = GROWS["kb"] + 1
        assert NGR <= P
        grow = sb("grow", [NGR, P])
        gain = sb("gain", [P, NGR])
        ssq = sb("ssq", [P, 9, TT, 4])
        rstd = sb("rstd", [P, 9, TT])
        gsc = sb("gsc", [P, 4, TT])
        ksum = sb("ksum", [P, TT])
        kmean = sb("kmean", [P, TT])
        widx = sb("widx", [P, TT, IH])
        max8 = sb("max8", [P, TT, 8])
        lmax = sb("lmax", [P, 2, TT])
        lsum = sb("lsum", [P, 2, TT])
        linv = sb("linv", [P, 2, TT])

        def gcol(name, k):
            return gain[:, GROWS[name] + k:GROWS[name] + k + 1]

        def place(off, name, shape, dt=F32):
            with ExitStack() as s:
                if off:
                    s.enter_context(nc.sbuf_tensor(f"pad_{name}", [P, off // 4], F32))
                return s.enter_context(nc.sbuf_tensor(name, shape, dt))

        KB = 1024
        H = 0
        h_hi = place(H, "h_hi", [P, KD, T], F32R)
        h_lo = place(H + 16 * KB, "h_lo", [P, KD, T], F32R)
        uk = place(H, "uk", [P, KC, NH, HD])
        uv = place(H + 12 * KB, "uv", [P, KC, NH, HD])
        kT = place(H + 12 * KB, "kT", [P, NH, T])
        qidxT = place(H + 24 * KB, "qidxT", [P, IH // 2, T])
        gfin = place(H, "gfin", [P, D])
        M = H + 32 * KB
        mix_hi = place(M, "mix_hi", [P, KD, T], F32R)
        mix_lo = place(M + 16 * KB, "mix_lo", [P, KD, T], F32R)
        acc = place(M, "acc", [P, TT, T])
        work = place(M + 2 * KB, "work", [P, TT, T])
        relus = place(M + 4 * KB, "relus", [P, 2, TT, T])
        kdup = place(M + 8 * KB, "kdup", [P, TT, 2, ID])
        m = M + 32 * KB
        lg = place(m, "lg", [P, 2, TT, T])
        cq_hi = place(m, "cq_hi", [P, KQ, T], F32R)
        pT = place(m + 4 * KB, "pT", [P, 2, TT, T])
        cq_lo = place(m + 4 * KB, "cq_lo", [P, KQ, T], F32R)
        qmemT = place(m + 8 * KB, "qmemT", [P, MH, T])
        m += 12 * KB
        proj = place(m, "proj", [P, TT, ATTN_IN])
        n = m + 11 * KB
        ckvT = place(n, "ckvT", [P, KC, T])
        kidxT = place(n + 2 * KB, "kidxT", [P, T])
        maskb = place(n + 3 * KB, "maskb", [P, TT, T])
        mk0T = place(n + 5 * KB, "mk0T", [P, MH, T])
        mv0 = place(n + 9 * KB, "mv0", [P, TT, MW])
        qT = place(n + 13 * KB, "qT", [P, NH, T])
        v = place(n + 25 * KB, "v", [P, TT, NH * HD])
        memt = place(n + 13 * KB, "memt", [P, TT, D])
        u1 = place(m, "u1", [P, TT, D])
        yT = place(m + 16 * KB, "yT", [P, PW // P, T])
        wg = place(m + 28 * KB, "wg", [P, NG, KG, PG])
        bandA = place(m + 46 * KB, "bandA", [P, NG, T])
        bandC = place(m + 50 * KB, "bandC", [P, NG, P])
        rcnt = place(m + 52 * KB, "rcnt", [P, T])
        hid_hi = place(M, "hid_hi", [P, KF, T], F32R)
        hid_lo = place(M + KF * KB, "hid_lo", [P, KF, T], F32R)

        psum = ctx.enter_context(nc.psum_tensor("psum", [P, 4 + NBANK, NW], F32))
        bank = [psum[:, 4 + b, :] for b in range(NBANK)]

        raw_in = [sem(f"raw_in{s}") for s in range(RING)]
        hi_ready = sem("hi_ready")
        lo_ready = sem("lo_ready")
        tile_used = sem("tile_used")
        taken = [sem("takenA"), sem("takenB")]
        job_done = sem("job_done")
        emptied = [sem(f"emptied{b}") for b in range(NBANK)]
        tr_hi = sem("tr_hi")
        mem_in = [sem(f"mem_in{q}") for q in range(4)]
        x_in = sem("x_in")
        gains_in = sem("gains_in")
        ukv_in = sem("ukv_in")
        wg_in = sem("wg_in")
        gfin_in = sem("gfin_in")
        ident_ready = sem("ident_ready")
        ssq_ready = sem("ssq_ready")
        rstd_ready = sem("rstd_ready")
        pool_seq = sem("pool_seq")
        dve_seq = sem("dve_seq")
        x_new = sem("x_new")
        cq_normed = sem("cq_normed")
        kidx_centred = sem("kidx_centred")
        kv_normed = sem("kv_normed")
        scored = sem("scored")
        causal = sem("causal")
        mask_raw = sem("mask_raw")
        lg_ready = sem("lg_ready")
        exp_done = sem("exp_done")
        p_ready = sem("p_ready")
        counts_ready = sem("counts_ready")
        rcnt_ready = sem("rcnt_ready")
        bands_ready = sem("bands_ready")
        out_piece = sem("out_piece")
        out_done = sem("out_done")

        MEM, X0, CQ, CKV, KIDX, F0, X1, F1, FIN = range(9)
        FFN_NORM, IN_NORM = (F0, F1), (X0, X1)

        def fp(ap):
            return ap.bitcast(F32)

        def wait_chunk(eng, c):
            eng.wait_ge(tile_used, LAST[c] + 1)

        def wait_taken(eng, c):
            eng.wait_ge(taken[c % 2], c // 2 + 1)

        def wait_emptied(eng, j):
            eng.wait_ge(emptied[j % NBANK], j // NBANK + 1)

        def chunk_width(c):
            return ATTN_IN - 2 * NW if c == CHUNK["in0"] + 2 else NW

        def tile_width(t):
            return ATTN_IN - 2 * NW if LAST[CHUNK["in0"] + 1] < t <= LAST[CHUNK["in0"] + 2] else NW

        block = ctx.enter_context(nc.Block())

        @block.sync
        def _(sp):
            memv = mem.rearrange("b (t p) d -> p (b t) d", p=P)
            for q in range(4):
                sp.dma_start(memt[:, :, q * NW:(q + 1) * NW], memv[:, :, q * NW:(q + 1) * NW]).then_inc(mem_in[q], 16)

            def load(w, k, cols, t, more=0):
                if t >= RING:
                    sp.wait_ge(lo_ready, more + (t - RING + 1))
                src = w.rearrange("(k p) n -> p k n", p=P)[:, 2 * k:2 * k + 2, cols]
                sp.dma_start(raw[:, t % RING, :, 0:src.shape[2]], src).then_inc(raw_in[t % RING], 16)

            def product(name, w, per, chunks):
                for c in range(chunks):
                    for k in range(per):
                        load(w, k, slice(c * NW, min((c + 1) * NW, w.shape[1])), TILE[name] + c * per + k)

            def product_loop(name, w, per):
                with sp.Fori(0, D // NW // 2) as i:
                    for half in range(2):
                        for k in range(per):
                            load(w, k, bass.ds(i * (2 * NW) + half * NW, NW), TILE[name] + half * per + k, i * (2 * per))

            for k in range(2 * CT_D):
                if k == RING:
                    sp.dma_start(xres[:, :, :], x.rearrange("b (t p) d -> p (b t) d", p=P)).then_inc(x_in, 16)
                load(w_mem_kv[0], k % CT_D, slice(k // CT_D * NW, (k // CT_D + 1) * NW), TILE["mem0"] + k)
            product("mem1", w_mem_kv[1], CT_D, 2)
            product("in0", w_in_attn[0], CT_D, 3)
            product("idx", w_idx_uq[0], CT_Q, 2)
            product("uq", w_uq[0], CT_Q, 3)
            for layer in range(LAYERS):
                if layer:
                    product("in1", w_in_pool[0], CT_D, 4)
                product_loop(f"out{layer}", w_out[layer], CT_D)
                with sp.Fori(0, FFN_IT) as i:
                    for half, w in ((0, w_gate), (1, w_up)):
                        for k in range(CT_D):
                            load(w[layer], k, bass.ds(i * NW, NW), TILE[f"ffn{layer}"] + half * CT_D + k, i * (2 * CT_D))
                product_loop(f"down{layer}", w_down[layer], CT_F)

            sp.wait_ge(tile_used, TILE["down1"])
            sp.dma_start(gfin[:, :], final_norm.partition_broadcast(P)).then_inc(gfin_in, 16)
            outv = out.rearrange("b (t p) d -> p (b t) d", p=P)
            for piece in range(2 * TT):
                sp.wait_ge(out_piece, piece + 1)
                tt, c0 = piece // 2, piece % 2 * (D // 2)
                sp.dma_start(outv[:, tt, c0:c0 + D // 2], xres[:, tt, c0:c0 + D // 2]).then_inc(out_done, 16)
            sp.wait_ge(out_done, 16 * 2 * TT)

        @block.gpsimd
        def _(pool):
            seq = [0]

            def step(ins):
                seq[0] += 1
                ins.then_inc(pool_seq, 1)
                pool.wait_ge(pool_seq, seq[0])

            step(pool.memset(ident[:, :], 0.0))
            pool.affine_select(out=ident[:, :], in_=ident[:, :], compare_op=ALU.not_equal, fill=1.0, base=0,
                               pattern=[[-1, P]], channel_multiplier=1).then_inc(ident_ready, 1)
            step(pool.memset(gsc[:, 3, :], -0.5))

            def rstd_of(n, width, parts):
                s = ssq[:, n, :, :]
                if parts == 4:
                    step(pool.tensor_tensor(s[:, :, 0:2], s[:, :, 0:2], s[:, :, 2:4], ALU.add))
                    step(pool.tensor_tensor(s[:, :, 0:1], s[:, :, 0:1], s[:, :, 1:2], ALU.add))
                var, est, sq = gsc[:, 0, :], gsc[:, 1, :], gsc[:, 2, :]
                step(pool.tensor_scalar(var, s[:, :, 0], 1.0 / width, EPS, ALU.mult, ALU.add))
                step(pool.tensor_tensor(est, var, gsc[:, 3, :], ALU.pow))
                step(pool.tensor_tensor(sq, est, est, ALU.mult))
                step(pool.tensor_tensor(sq, sq, var, ALU.mult))
                step(pool.tensor_scalar(sq, sq, -0.5, 1.5, ALU.mult, ALU.add))
                pool.tensor_tensor(rstd[:, n, :], est, sq, ALU.mult).then_inc(rstd_ready, 1)
                pool.wait_ge(rstd_ready, n + 1)

            pool.wait_ge(ssq_ready, MEM + 1)
            rstd_of(MEM, D, 4)
            pool.wait_ge(ssq_ready, X0 + 1)
            rstd_of(X0, D, 4)
            pool.wait_ge(ssq_ready, CQ + 1)
            rstd_of(CQ, QL, 1)
            pool.wait_ge(ssq_ready, CKV + 1)
            rstd_of(CKV, KVL, 1)
            pool.wait_ge(tile_used, TILE["idx"])
            for ct in range(KC):
                pool.dma_start(uk[:, ct, :, :], w_uk[0, :, ct * P:(ct + 1) * P, :].rearrange("h c d -> c h d")).then_inc(ukv_in, 16)
                pool.dma_start(uv[:, ct, :, :], w_uv[0, :, ct * P:(ct + 1) * P, :].rearrange("h c d -> c h d")).then_inc(ukv_in, 16)
            pool.wait_ge(ssq_ready, KIDX + 1)
            rstd_of(KIDX, ID, 1)
            pool.wait_ge(scored, TT * IH)
            for qb in range(TT):
                pool.affine_select(out=work[:, qb, :], in_=acc[:, qb, :], compare_op=ALU.is_ge, fill=NONCAUSAL,
                                   base=qb * P, pattern=[[-1, T]], channel_multiplier=1).then_inc(causal, 1)
            for qb in range(TT):
                pool.wait_ge(mask_raw, qb + 1)
                pool.affine_select(out=maskb[:, qb, :], in_=maskb[:, qb, :], compare_op=ALU.is_ge, fill=MASKED,
                                   base=qb * P, pattern=[[-1, T]], channel_multiplier=1).then_inc(causal, 1)
            wait_taken(pool, CHUNK["out0"] + 3)
            rstd_of(F0, D, 4)
            pool.wait_ge(tile_used, TILE["in1"])
            for g in range(NG):
                pool.dma_start(wg[:, g, :, :], w_pool_group[0, g].rearrange("(k p) d -> p k d", p=P)).then_inc(wg_in, 16)
            wait_taken(pool, CHUNK["down0"] + 3)
            rstd_of(X1, D, 4)
            counts = bandA[:, 0, :].bitcast(mybir.dt.int32)
            step(pool.iota(counts, pattern=[[1, T]], base=1, channel_multiplier=0))
            pool.tensor_copy(rcnt[:, :], counts).then_inc(counts_ready, 1)
            pool.wait_ge(rcnt_ready, 1)
            for g in range(NG):
                win = 2 ** (g + 1)
                step(pool.tensor_scalar(bandA[:, g, :], rcnt[:, :], 1.0 / win, None, ALU.max))
                step(pool.memset(bandC[:, g, :], 1.0 / win))
                for band, width in ((bandA, T), (bandC, P)):
                    step(pool.affine_select(out=band[:, g, :], in_=band[:, g, :], compare_op=ALU.is_ge, fill=0.0,
                                            base=0, pattern=[[1, width]], channel_multiplier=-1))
                    step(pool.affine_select(out=band[:, g, :], in_=band[:, g, :], compare_op=ALU.is_ge, fill=0.0,
                                            base=win - 1, pattern=[[-1, width]], channel_multiplier=1))
                    pool.tensor_tensor(band[:, g, 0:P], band[:, g, 0:P], ident[:, :], ALU.subtract).then_inc(bands_ready, 1)
            wait_taken(pool, CHUNK["out1"] + 3)
            rstd_of(F1, D, 4)
            wait_taken(pool, CHUNK["down1"] + 3)
            rstd_of(FIN, D, 4)

        @block.scalar
        def _(act):
            def convert(t, more=0):
                s, w = t % RING, tile_width(t)
                act.wait_ge(raw_in[s], more * (16 // RING) + 16 * (t // RING + 1))
                if t >= RING:
                    act.wait_ge(tile_used, more + (t - RING + 1))
                act.activation(whi[:, s, :, 0:w], raw[:, s, :, 0:w], ACT.Copy).then_inc(hi_ready, 1)

            nxt = [0]

            def convert_until(end):
                while nxt[0] < min(end, TILES):
                    convert(nxt[0])
                    nxt[0] += 1

            def hi_of(job, dst, scale):
                act.wait_ge(job_done, job + 1)
                act.activation(dst, bank[job % NBANK][:, 0:T], ACT.Copy, scale=scale).then_inc(tr_hi, 1)

            def fill(job0, tile0, dst, name, k_first):
                for n, k0 in enumerate(FILL_BEFORE.values()):
                    for k in range(k0, k0 + 4):
                        hi_of(job0 + k, dst[:, k, :], gcol(name, k_first + k))
                    if n < 3:
                        convert_until(tile0 + AHEAD + n + 1)

            def squares(src, junk, norm, part):
                for tt in range(TT):
                    ins = act.activation(junk(tt), src(tt), ACT.Square, accum_out=ssq[:, norm, tt, part])
                return ins

            def take(c, dst, c0, norm=None):
                w = chunk_width(c)
                wait_chunk(act, c)
                if norm is not None:
                    act.wait_ge(rstd_ready, norm + 1)
                for tt in range(TT):
                    ins = act.activation(dst[:, tt, c0:c0 + w], psum[:, 2 * (c % 2) + tt, 0:w], ACT.Copy,
                                         scale=1.0 if norm is None else rstd[:, norm, tt:tt + 1])
                ins.then_inc(taken[c % 2], 1)

            def pair(c, tt, a, b):
                return psum[:, 2 * (c % 2) + tt, a:b]

            g1 = lambda ap: ap.rearrange("(k p) -> k p", p=P)
            for l in range(LAYERS):
                act.dma_start(grow[GROWS["mix"] + l * KD:GROWS["mix"] + (l + 1) * KD, :], g1(mixer_norm[l])).then_inc(gains_in, 16)
                act.dma_start(grow[GROWS["ffn"] + l * KD:GROWS["ffn"] + (l + 1) * KD, :], g1(ffn_norm[l])).then_inc(gains_in, 16)
            for name, src, rows in (("mem", mem_norm, KD), ("q", q_norm[0], KQ), ("kv", kv_norm[0], KC),
                                    ("pool", pool_scale[0], PW // P)):
                act.dma_start(grow[GROWS[name]:GROWS[name] + rows, :], g1(src)).then_inc(gains_in, 16)
            for name, src in (("ki", idx_k_norm), ("kb", idx_k_bias)):
                for h in range(2):
                    act.dma_start(grow[GROWS[name]:GROWS[name] + 1, h * ID:(h + 1) * ID], src).then_inc(gains_in, 16)

            convert_until(AHEAD)
            wait_emptied(act, JOB["gains"])
            fill(JOB["memT"], TILE["mem0"], mix_hi, "mem", 0)
            act.wait_ge(job_done, JOB["memT"] + KD)
            for q in range(4):
                ins = squares(lambda tt: memt[:, tt, q * NW:(q + 1) * NW], lambda tt: memt[:, tt, q * NW:(q + 1) * NW], MEM, slice(q, q + 1))
            ins.then_inc(ssq_ready, 1)
            c = CHUNK["mem0"]
            convert_until(LAST[c] + 1 + AHEAD)
            take(c, stage, 0, MEM)
            act.wait_ge(x_in, 16)
            act.wait_ge(ssq_ready, MEM + 1)
            for q in range(4):
                ins = squares(lambda tt: xres[:, tt, q * NW:(q + 1) * NW], lambda tt: memt[:, tt, q * NW:(q + 1) * NW], X0, slice(q, q + 1))
            ins.then_inc(ssq_ready, 1)
            convert_until(LAST[c + 1] + 1 + AHEAD)
            take(c + 1, mv0, 0, MEM)
            c = CHUNK["mem1"]
            convert_until(LAST[c] + 1 + AHEAD)
            act.wait_ge(job_done, JOB["mk0"] + MH)
            take(c, stage, 0, MEM)
            convert_until(LAST[c + 1] + 1 + AHEAD)
            take(c + 1, mv1, 0, MEM)

            fill(JOB["h0"], TILE["in0"], h_hi, "mix", 0)
            c = CHUNK["in0"]
            convert_until(LAST[c] + 1 + AHEAD)
            wait_chunk(act, c)
            act.wait_ge(rstd_ready, X0 + 1)
            act.wait_ge(job_done, JOB["mk1"] + MH)
            for tt in range(TT):
                ins = act.activation(stage[:, tt, 0:QL], pair(c, tt, 0, QL), ACT.Square, scale=rstd[:, X0, tt:tt + 1],
                                     accum_out=ssq[:, CQ, tt, 0:1])
            ins.then_inc(ssq_ready, 1)
            take(c, proj, 0, X0)
            convert_until(TILE["in0"] + CT_D + 6)
            for k in range(KQ):
                hi_of(JOB["cq"] + k, cq_hi[:, k, :], gcol("q", k))
            c += 1
            convert_until(LAST[c] + 1 + AHEAD)
            wait_chunk(act, c)
            act.wait_ge(ssq_ready, CQ + 1)
            for tt in range(TT):
                act.activation(stage[:, tt, 0:ID], pair(c, tt, C_KI - NW, C_WI - NW), ACT.Copy, scale=rstd[:, X0, tt:tt + 1],
                               accum_out=ksum[:, tt:tt + 1])
                ins = act.activation(stage[:, tt, ID:ID + KVL], pair(c, tt, 0, KVL), ACT.Square,
                                     scale=rstd[:, X0, tt:tt + 1], accum_out=ssq[:, CKV, tt, 0:1])
            ins.then_inc(ssq_ready, 1)
            take(c, proj, NW, X0)
            convert_until(LAST[c + 1] + 1 + AHEAD)
            take(c + 1, proj, 2 * NW, X0)
            act.wait_ge(kidx_centred, TT)
            for tt in range(TT):
                ins = act.activation(kdup[:, tt, 1, :], kdup[:, tt, 0, :], ACT.Square, accum_out=ssq[:, KIDX, tt, 0:1])
            ins.then_inc(ssq_ready, 1)
            c = CHUNK["idx"]
            convert_until(LAST[c] + 1 + AHEAD)
            act.wait_ge(ssq_ready, KIDX + 1)
            take(c, stage, 0)
            convert_until(LAST[c + 1] + 1 + AHEAD)
            take(c + 1, proj, 0)
            act.wait_ge(job_done, JOB["kidx"] + 1)
            act.activation(kidxT[:, :], bank[JOB["kidx"] % NBANK][:, 0:T], ACT.Identity, scale=gcol("ki", 0),
                           bias=gcol("kb", 0)).then_inc(emptied[JOB["kidx"] % NBANK], 1)
            c = CHUNK["uq"]
            for part, (dst, before) in enumerate(((stage, "qidx0"), (proj, "qidx1"), (stage, "q0"))):
                convert_until(LAST[c + part] + 1 + AHEAD)
                act.wait_ge(job_done, JOB[before] + KPC)
                take(c + part, dst, 0)
            for h in range(IH):
                j = JOB["score"] + h
                act.wait_ge(job_done, j + 1)
                if h >= 2:
                    act.wait_ge(scored, TT * (h - 1))
                act.activation(relus[:, h % 2, :, :], bank[j % NBANK].rearrange("p (q s) -> p q s", q=TT),
                               ACT.Relu).then_inc(emptied[j % NBANK], 1)
            for hp in range(NH // 2):
                j = JOB["k"] + hp
                act.wait_ge(job_done, j + 1)
                act.activation(kT[:, 2 * hp:2 * hp + 2, :], bank[j % NBANK].rearrange("p (h s) -> p h s", h=2),
                               ACT.Copy).then_inc(emptied[j % NBANK], 1)

            def attend(layer):
                number, order = head_jobs(layer), heads(layer)
                before = len(heads(0)) * layer
                for s in range(len(order) + 2):
                    if s < len(order):
                        act.wait_ge(lg_ready, before + s + 1)
                        for qb in range(TT):
                            ins = act.activation(lg[:, s % 2, qb, :], lg[:, s % 2, qb, :], ACT.Exp,
                                                 bias=lmax[:, s % 2, qb:qb + 1], accum_out=lsum[:, s % 2, qb:qb + 1])
                        ins.then_inc(exp_done, 1)
                    if 0 <= s - 1 < len(order):
                        j = number["probs", s - 1]
                        act.wait_ge(job_done, j + 1)
                        if s - 1 >= 2:
                            act.wait_ge(job_done, number["output", s - 3] + 1)
                        act.activation(pT[:, (s - 1) % 2, :, :], bank[j % NBANK].rearrange("p (a q) -> p a q", a=TT),
                                       ACT.Copy).then_inc(emptied[j % NBANK], 1)
                    if 0 <= s - 2:
                        hi_of(number["output", s - 2], mix_hi[:, kt_of(*order[s - 2]), :], 1.0)

            def residual(name, per, norm):
                c0, t0 = CHUNK[name], TILE[name]
                if TILES - t0 == 4 * per:
                    for n in range(D // NW):
                        convert_until(LAST[c0 + n] + 1 + AHEAD)
                        act.wait_ge(x_new, X_CHUNKS[name] + n + 1)
                        squares(lambda tt: xres[:, tt, n * NW:(n + 1) * NW], lambda tt: pair(c0 + n, tt, 0, NW), norm,
                                slice(n, n + 1)).then_inc(taken[n % 2], 1)
                    return
                with act.Fori(0, D // NW // 2) as i:
                    for half in range(2):
                        for k in range(per):
                            convert(t0 + AHEAD + half * per + k, i * (2 * per))
                        act.wait_ge(x_new, i * 2 + (X_CHUNKS[name] + half + 1))
                        squares(lambda tt: xres[:, tt, bass.ds(i * (2 * NW) + half * NW, NW)],
                                lambda tt: pair(half, tt, 0, NW), norm, bass.ds(i * 2 + half, 1)).then_inc(taken[half], 1)
                nxt[0] += 4 * per

            def ffn(layer):
                t0, c0, job0, norm = TILE[f"ffn{layer}"], CHUNK[f"ffn{layer}"], JOB[f"hid{layer}"], FFN_NORM[layer]

                def silu(more):
                    act.wait_ge(tile_used, more + (LAST[c0] + 1))
                    act.wait_ge(rstd_ready, norm + 1)
                    for tt in range(TT):
                        ins = act.activation(stage[:, tt, :], pair(c0, tt, 0, NW), ACT.Silu, scale=rstd[:, norm, tt:tt + 1])
                    ins.then_inc(taken[0], 1)

                def hidden(kt):
                    for k in range(KPC):
                        j = job0 + k
                        act.wait_ge(job_done, kt + (j + 1))
                        act.activation(hid_hi[:, bass.ds(kt + k, 1), :].rearrange("p a t -> p (a t)"),
                                       bank[j % NBANK][:, 0:T], ACT.Copy).then_inc(tr_hi, 1)

                fill(JOB[f"f{layer}"], t0, h_hi, "ffn", layer * KD)
                convert_until(LAST[c0] + 1 + AHEAD)
                silu(0)
                convert_until(LAST[c0 + 1] + 1 + AHEAD)
                hidden(0)
                with act.Fori(1, FFN_IT) as i:
                    for k in range(CT_D):
                        convert(t0 + AHEAD + k, i * (2 * CT_D))
                    silu(i * (2 * CT_D))
                    for k in range(CT_D, 2 * CT_D):
                        convert(t0 + AHEAD + k, i * (2 * CT_D))
                    hidden(i * KPC)
                nxt[0] += 2 * CT_D * (FFN_IT - 1)

            attend(0)
            residual("out0", CT_D, F0)
            ffn(0)
            residual("down0", CT_F, X1)

            fill(JOB["h1"], TILE["in1"], h_hi, "mix", KD)
            c = CHUNK["in1"]

            def group(job0, number):
                for n in range(number):
                    kt = n + (KG if job0 == JOB["group123"] else 0)
                    hi_of(job0 + n, mix_hi[:, kt, :], gcol("pool", kt))

            for n in range(2):
                convert_until(LAST[c + n] + 1 + AHEAD)
                take(c + n, u1, n * NW, X1)
            convert_until(LAST[c + 1] + 1 + 7)
            group(JOB["group0"], KG)
            for n in range(2, 4):
                convert_until(LAST[c + n] + 1 + AHEAD)
                take(c + n, u1, n * NW, X1)
            group(JOB["group123"], 3 * KG)
            attend(1)
            residual("out1", CT_D, F1)
            ffn(1)
            residual("down1", CT_F, FIN)

        @block.vector
        def _(dve):
            seq = [0]

            def did(ins):
                seq[0] += 1
                ins.then_inc(dve_seq, 1)
                return seq[0]

            def convert(t, more=0):
                s, w = t % RING, tile_width(t)
                dve.wait_ge(hi_ready, more + (t + 1))
                dve.tensor_tensor(wlo[:, s, :, 0:w], raw[:, s, :, 0:w], fp(whi[:, s, :, 0:w]), ALU.subtract).then_inc(lo_ready, 1)

            nxt = [0]

            def convert_until(end):
                while nxt[0] < min(end, TILES):
                    convert(nxt[0])
                    nxt[0] += 1

            def lo_of(job, tr, dst, hi, scale):
                dve.wait_ge(tr_hi, tr + 1)
                dve.scalar_tensor_tensor(out=dst, in0=bank[job % NBANK][:, 0:T], scalar=scale, in1=fp(hi), op0=ALU.mult,
                                         op1=ALU.subtract).then_inc(emptied[job % NBANK], 1)

            def fill(job0, tr0, tile0, dst, hi, name, k_first):
                for n, k0 in enumerate(FILL_BEFORE.values()):
                    for k in range(k0, k0 + 4):
                        lo_of(job0 + k, tr0 + k, dst[:, k, :], hi[:, k, :], gcol(name, k_first + k))
                    if n < 3:
                        convert_until(tile0 + AHEAD + n + 1)

            def copy_of(job, dst):
                dve.wait_ge(job_done, job + 1)
                dve.tensor_copy(dst, bank[job % NBANK][:, 0:T]).then_inc(emptied[job % NBANK], 1)

            dve.wait_ge(job_done, JOB["gains"] + 1)
            dve.tensor_copy(gain[:, :], bank[JOB["gains"] % NBANK][:, 0:NGR]).then_inc(emptied[JOB["gains"] % NBANK], 1)
            wait_emptied(dve, JOB["gains"])
            convert_until(AHEAD)
            fill(JOB["memT"], TR["memT"], TILE["mem0"], mix_lo, mix_hi, "mem", 0)
            for l, dst in ((0, mk0T), (1, mk1T)):
                convert_until(LAST[CHUNK[f"mem{l}"] + 1] - CT_D + 1 + 5)
                for h in range(MH):
                    copy_of(JOB[f"mk{l}"] + h, dst[:, h, :])

            convert_until(TILE["in0"] + AHEAD)
            fill(JOB["h0"], TR["h0"], TILE["in0"], h_lo, h_hi, "mix", 0)
            c = CHUNK["in0"]
            convert_until(LAST[c] + 1 + 4)
            wait_taken(dve, c)
            dve.wait_ge(rstd_ready, CQ + 1)
            for tt in range(TT):
                dve.tensor_scalar(proj[:, tt, 0:QL], proj[:, tt, 0:QL], rstd[:, CQ, tt:tt + 1], None, ALU.mult).then_inc(cq_normed, 1)
            convert_until(LAST[c] + 1 + 6)
            for k in range(KQ):
                lo_of(JOB["cq"] + k, TR["cq"] + k, cq_lo[:, k, :], cq_hi[:, k, :], gcol("q", k))
            convert_until(LAST[c + 1] + 1 + AHEAD)
            wait_taken(dve, c + 1)
            n = did(dve.tensor_scalar(kmean[:, :], ksum[:, :], -1.0 / ID, None, ALU.mult))
            dve.wait_ge(dve_seq, n)
            for tt in range(TT):
                dve.tensor_scalar(kdup[:, tt, 0, :], proj[:, tt, C_KI:C_WI], kmean[:, tt:tt + 1], None, ALU.add).then_inc(kidx_centred, 1)
            convert_until(LAST[c + 2] + 1 + AHEAD)
            dve.tensor_scalar(widx[:, :, :], proj[:, :, C_WI:C_QM], IH ** -0.5 * ID ** -0.5, None, ALU.mult)
            dve.wait_ge(rstd_ready, CKV + 1)
            for tt in range(TT):
                dve.tensor_scalar(proj[:, tt, C_KV:C_KI], proj[:, tt, C_KV:C_KI], rstd[:, CKV, tt:tt + 1], None, ALU.mult).then_inc(kv_normed, 1)
            dve.wait_ge(rstd_ready, KIDX + 1)
            for tt in range(TT):
                dve.tensor_scalar(kdup[:, tt, 1, :], kdup[:, tt, 0, :], rstd[:, KIDX, tt:tt + 1], None, ALU.mult).then_inc(kv_normed, 1)
                dve.tensor_scalar(kdup[:, tt, 0, :], kdup[:, tt, 0, :], rstd[:, KIDX, tt:tt + 1], None, ALU.mult).then_inc(kv_normed, 1)
            convert_until(LAST[CHUNK["idx"] + 1] + 1 + AHEAD)
            for k in range(KC):
                dve.wait_ge(job_done, JOB["ckv"] + k + 1)
                dve.tensor_scalar(ckvT[:, k, :], bank[(JOB["ckv"] + k) % NBANK][:, 0:T], gcol("kv", k), None,
                                  ALU.mult).then_inc(emptied[(JOB["ckv"] + k) % NBANK], 1)
            for h in range(MH):
                copy_of(JOB["qmem0"] + h, qmemT[:, h, :])
            c = CHUNK["uq"]
            for k in range(KPC):
                copy_of(JOB["qidx0"] + k, qidxT[:, k, :])
            convert_until(LAST[c] + 1 + AHEAD)
            for k in range(KPC):
                copy_of(JOB["qidx1"] + k, qidxT[:, KPC + k, :])
            convert_until(LAST[c + 1] + 1 + AHEAD)
            for k in range(KPC):
                copy_of(JOB["q0"] + k, qT[:, k, :])
            convert_until(LAST[c + 2] + 1 + AHEAD)
            for h in range(IH):
                wait_emptied(dve, JOB["score"] + h)
                for qb in range(TT):
                    w = widx[:, qb, h:h + 1]
                    if h == 0:
                        dve.tensor_scalar(acc[:, qb, :], relus[:, 0, qb, :], w, None, ALU.mult).then_inc(scored, 1)
                    else:
                        dve.wait_ge(scored, TT * (h - 1) + qb + 1)
                        dve.scalar_tensor_tensor(out=acc[:, qb, :], in0=relus[:, h % 2, qb, :], scalar=w, in1=acc[:, qb, :],
                                                 op0=ALU.mult, op1=ALU.add).then_inc(scored, 1)
            for n in range(2):
                for k in range(KPC):
                    copy_of(JOB[f"q{n + 1}"] + k, qT[:, (n + 1) * KPC + k, :])
            for j in range(TT * NH // 4):
                dve.wait_ge(job_done, JOB["v"] + j + 1)
                st, hc = j % TT, j // TT
                dve.tensor_copy(v[:, st, hc * NW:(hc + 1) * NW], bank[(JOB["v"] + j) % NBANK]).then_inc(emptied[(JOB["v"] + j) % NBANK], 1)

            def select():
                written = [None, None]
                for r in range(TOPK // 8):
                    best = []
                    for qb in range(TT):
                        if r == 0:
                            dve.wait_ge(causal, qb + 1)
                        else:
                            dve.wait_ge(dve_seq, written[qb])
                        best.append(did(dve.max(out=max8[:, qb, :], in_=work[:, qb, :])))
                    for qb in range(TT):
                        dve.wait_ge(dve_seq, best[qb])
                        written[qb] = did(dve.match_replace(out=work[:, qb, :], in_to_replace=max8[:, qb, :],
                                                            in_values=work[:, qb, :], imm_value=TAKEN))
                for qb in range(TT):
                    dve.wait_ge(dve_seq, written[qb])
                    dve.tensor_scalar(maskb[:, qb, :], work[:, qb, :], TAKEN_BELOW, MASKED, ALU.is_gt, ALU.mult).then_inc(mask_raw, 1)

            def attend(layer):
                number, order = head_jobs(layer), heads(layer)
                before = len(heads(0)) * layer
                for s in range(len(order) + 2):
                    if s < len(order):
                        is_self, h = order[s]
                        if is_self and h == 0:
                            dve.wait_ge(causal, 2 * TT)
                        r, j = s % 2, number["logits", s]
                        dve.wait_ge(job_done, j + 1)
                        if s >= 2:
                            dve.wait_ge(job_done, number["probs", s - 2] + 1)
                        src = bank[j % NBANK].rearrange("p (q s) -> p q s", q=TT)
                        if is_self:
                            ins = dve.scalar_tensor_tensor(out=lg[:, r, :, :], in0=src, scalar=SCALE, in1=maskb[:, :, :],
                                                           op0=ALU.mult, op1=ALU.add)
                        else:
                            ins = dve.tensor_scalar(lg[:, r, :, :], src, SCALE, None, ALU.mult)
                        ins.then_inc(emptied[j % NBANK], 1)
                        wait_emptied(dve, j)
                        dve.tensor_reduce(out=lmax[:, r, :], in_=lg[:, r, :, :], axis=AX.X, op=ALU.max, negate=True).then_inc(lg_ready, 1)
                    if 0 <= s - 1 < len(order):
                        r = (s - 1) % 2
                        dve.wait_ge(exp_done, before + s)
                        dve.wait_ge(dve_seq, did(dve.reciprocal(linv[:, r, :], lsum[:, r, :])))
                        for qb in range(TT):
                            ins = dve.tensor_scalar(lg[:, r, qb, :], lg[:, r, qb, :], linv[:, r, qb:qb + 1], None, ALU.mult)
                        ins.then_inc(p_ready, 1)
                    if 0 <= s - 2:
                        kt = kt_of(*order[s - 2])
                        lo_of(number["output", s - 2], TR[f"head{layer}"] + s - 2, mix_lo[:, kt, :], mix_hi[:, kt, :], 1.0)

            def residual(name, per):
                c0, t0 = CHUNK[name], TILE[name]
                if TILES - t0 == 4 * per:
                    for n in range(D // NW):
                        convert_until(LAST[c0 + n] + 1 + AHEAD)
                        wait_chunk(dve, c0 + n)
                        dve.tensor_tensor(xres[:, :, n * NW:(n + 1) * NW], xres[:, :, n * NW:(n + 1) * NW],
                                          psum[:, 2 * (n % 2):2 * (n % 2) + 2, :], ALU.add).then_inc(x_new, 1)
                    return
                with dve.Fori(0, D // NW // 2) as i:
                    for half in range(2):
                        for k in range(per):
                            convert(t0 + AHEAD + half * per + k, i * (2 * per))
                        dve.wait_ge(tile_used, i * (2 * per) + (LAST[c0 + half] + 1))
                        cols = xres[:, :, bass.ds(i * (2 * NW) + half * NW, NW)]
                        dve.tensor_tensor(cols, cols, psum[:, 2 * half:2 * half + 2, :], ALU.add).then_inc(x_new, 1)
                nxt[0] += 4 * per

            def ffn(layer):
                t0, c0, job0, norm = TILE[f"ffn{layer}"], CHUNK[f"ffn{layer}"], JOB[f"hid{layer}"], FFN_NORM[layer]
                tr0 = TR[f"hid{layer}"]

                def up(i, more):
                    dve.wait_ge(tile_used, more + (LAST[c0 + 1] + 1))
                    dve.wait_ge(taken[0], i + (c0 // 2 + 1))
                    dve.wait_ge(rstd_ready, norm + 1)
                    for tt in range(TT):
                        ins = dve.scalar_tensor_tensor(out=stage[:, tt, :], in0=psum[:, 2 + tt, :], scalar=rstd[:, norm, tt:tt + 1],
                                                       in1=stage[:, tt, :], op0=ALU.mult, op1=ALU.mult)
                    ins.then_inc(taken[1], 1)

                def hidden(kt):
                    for k in range(KPC):
                        j = job0 + k
                        dve.wait_ge(tr_hi, kt + (tr0 + k + 1))
                        flat = lambda h: h[:, bass.ds(kt + k, 1), :].rearrange("p a t -> p (a t)")
                        dve.tensor_tensor(flat(hid_lo), bank[j % NBANK][:, 0:T], fp(flat(hid_hi)),
                                          ALU.subtract).then_inc(emptied[j % NBANK], 1)

                fill(JOB[f"f{layer}"], TR[f"f{layer}"], t0, h_lo, h_hi, "ffn", layer * KD)
                convert_until(LAST[c0 + 1] + 1 + AHEAD)
                up(0, 0)
                hidden(0)
                with dve.Fori(1, FFN_IT) as i:
                    for k in range(2 * CT_D):
                        convert(t0 + AHEAD + k, i * (2 * CT_D))
                    up(i, i * (2 * CT_D))
                    hidden(i * KPC)
                nxt[0] += 2 * CT_D * (FFN_IT - 1)

            select()
            attend(0)
            residual("out0", CT_D)
            ffn(0)
            residual("down0", CT_F)

            fill(JOB["h1"], TR["h1"], TILE["in1"], h_lo, h_hi, "mix", KD)
            dve.wait_ge(counts_ready, 1)
            dve.reciprocal(rcnt[:, :], rcnt[:, :]).then_inc(rcnt_ready, 1)
            c = CHUNK["in1"]

            def group(job0, tr0, number):
                for n in range(number):
                    kt = n + (KG if job0 == JOB["group123"] else 0)
                    lo_of(job0 + n, tr0 + n, mix_lo[:, kt, :], mix_hi[:, kt, :], gcol("pool", kt))

            convert_until(LAST[c + 1] + 1 + 5)
            for k in range(2 * KPC):
                copy_of(JOB["pool01"] + k, yT[:, k, :])
            convert_until(LAST[c + 1] + 1 + 7)
            group(JOB["group0"], TR["group0"], KG)
            convert_until(LAST[c + 2] + 1 + 5)
            for k in range(KPC):
                copy_of(JOB["pool2"] + k, yT[:, 2 * KPC + k, :])
            convert_until(LAST[c + 3] + 1 + AHEAD)
            group(JOB["group123"], TR["group123"], 3 * KG)
            for h in range(MH):
                copy_of(JOB["qmem1"] + h, qmemT[:, h, :])
            attend(1)
            residual("out1", CT_D)
            ffn(1)
            residual("down1", CT_F)

            dve.wait_ge(rstd_ready, FIN + 1)
            dve.wait_ge(gfin_in, 16)
            for piece in range(2 * TT):
                tt, c0 = piece // 2, piece % 2 * (D // 2)
                cols = xres[:, tt, c0:c0 + D // 2]
                dve.scalar_tensor_tensor(out=cols, in0=cols, scalar=rstd[:, FIN, tt:tt + 1], in1=gfin[:, c0:c0 + D // 2],
                                         op0=ALU.mult, op1=ALU.mult).then_inc(out_piece, 1)

        @block.tensor
        def _(pe):
            def products(t, n, hi, lo, p, tiles_in_chunk, more=0):
                w = tile_width(t)
                pe.wait_ge(lo_ready, more + (t + 1))
                for k in (2 * n, 2 * n + 1):
                    for tt in range(TT):
                        for a, b in ((hi, whi), (hi, wlo), (lo, whi)):
                            ins = pe.matmul(psum[:, 2 * p + tt, 0:w], a[:, k, tt * P:(tt + 1) * P], b[:, t % RING, k % 2, 0:w],
                                            start=(k == 0 and a is hi and b is whi),
                                            stop=(k == 2 * tiles_in_chunk - 1 and a is lo))
                ins.then_inc(tile_used, 1)

            def chunk(c, hi, lo, per, before={}):
                if c >= 2:
                    wait_taken(pe, c - 2)
                for n in range(per):
                    if n in before:
                        before[n]()
                    products(LAST[c] - per + 1 + n, n, hi, lo, c % 2, per)

            def bank_for(j):
                if j >= NBANK:
                    wait_emptied(pe, j - NBANK)
                return bank[j % NBANK]

            def transposed(j, src, k):
                b = bank_for(j)
                for tt in range(TT):
                    ins = pe.transpose(b[:, tt * P:(tt + 1) * P], src[:, tt, k * P:(k + 1) * P], ident[:, :])
                ins.then_inc(job_done, 1)

            def transposes(name, src, k0, number):
                for n in range(number):
                    transposed(JOB[name] + n, src, k0 + n)

            def fill_hooks(name, src, loaded=None):
                def hook(k0):
                    def run():
                        for k in range(k0, k0 + 4):
                            if loaded:
                                loaded(k)
                            transposed(JOB[name] + k, src, k)
                        if k0 == 0:
                            for k in range(4):
                                wait_emptied(pe, JOB[name] + k)
                    return run

                def settle(k0):
                    for k in range(k0, k0 + 4):
                        wait_emptied(pe, JOB[name] + k)
                hooks = {n: hook(k0) for n, k0 in FILL_BEFORE.items()}
                for k0 in (4, 8, 12):
                    inner = hooks.get(k0 // 2)
                    def run(inner=inner, k0=k0):
                        if inner:
                            inner()
                        settle(k0)
                    hooks[k0 // 2] = run
                return hooks

            pe.wait_ge(ident_ready, 1)
            pe.wait_ge(gains_in, 16 * (2 * LAYERS + 4 + 4))
            pe.transpose(bank_for(JOB["gains"])[:, 0:NGR], grow[:, :], ident[0:NGR, 0:NGR]).then_inc(job_done, 1)

            c = CHUNK["mem0"]
            chunk(c, mix_hi, mix_lo, CT_D, fill_hooks("memT", memt, lambda k: pe.wait_ge(mem_in[k * P // NW], 16)))

            def mem_keys(l):
                def run():
                    wait_taken(pe, CHUNK[f"mem{l}"])
                    transposes(f"mk{l}", stage, 0, MH)
                return run

            chunk(c + 1, mix_hi, mix_lo, CT_D, {4: mem_keys(0)})
            chunk(c + 2, mix_hi, mix_lo, CT_D)
            chunk(c + 3, mix_hi, mix_lo, CT_D, {4: mem_keys(1)})

            c = CHUNK["in0"]
            pe.wait_ge(x_in, 16)
            chunk(c, h_hi, h_lo, CT_D, fill_hooks("h0", xres))

            def latent_queries():
                pe.wait_ge(cq_normed, TT)
                transposes("cq", proj, 0, KQ)

            chunk(c + 1, h_hi, h_lo, CT_D, {5: latent_queries})
            chunk(c + 2, h_hi, h_lo, CT_D)
            for k in range(KQ):
                wait_emptied(pe, JOB["cq"] + k)
            c = CHUNK["idx"]
            chunk(c, cq_hi, cq_lo, CT_Q)
            chunk(c + 1, cq_hi, cq_lo, CT_Q)
            wait_taken(pe, CHUNK["in0"] + 2)
            pe.wait_ge(kv_normed, TT)
            transposes("ckv", proj[:, :, C_KV:C_KI], 0, KC)
            pe.wait_ge(kv_normed, 3 * TT)
            transposes("kidx", kdup[:, :, :, :].rearrange("p t a d -> p t (a d)"), 0, 1)
            transposes("qmem0", proj[:, :, C_QM:ATTN_IN], 0, MH)
            wait_taken(pe, c)
            transposes("qidx0", stage, 0, KPC)
            c = CHUNK["uq"]
            chunk(c, cq_hi, cq_lo, CT_Q)
            wait_taken(pe, c - 1)
            transposes("qidx1", proj, 0, KPC)
            chunk(c + 1, cq_hi, cq_lo, CT_Q)
            wait_taken(pe, c)
            transposes("q0", stage, 0, KPC)
            chunk(c + 2, cq_hi, cq_lo, CT_Q)
            wait_emptied(pe, JOB["kidx"])
            for k in range(KPC):
                wait_emptied(pe, JOB["qidx0"] + k)
                wait_emptied(pe, JOB["qidx1"] + k)
            for h in range(IH):
                b, r = bank_for(JOB["score"] + h), ID * (h % 2)
                for qb in range(TT):
                    ins = pe.matmul(b[:, qb * T:(qb + 1) * T], qidxT[r:r + ID, h // 2, qb * P:(qb + 1) * P],
                                    kidxT[r:r + ID, :], start=True, stop=True)
                ins.then_inc(job_done, 1)
            wait_taken(pe, c + 1)
            transposes("q1", proj, 0, KPC)
            wait_taken(pe, c + 2)
            transposes("q2", stage, 0, KPC)
            pe.wait_ge(ukv_in, 16 * 2 * KC)
            for k in range(KC):
                wait_emptied(pe, JOB["ckv"] + k)
            for j in range(TT * NH // 4):
                b, st, hc = bank_for(JOB["v"] + j), j % TT, j // TT
                for ct in range(KC):
                    ins = pe.matmul(b, ckvT[:, ct, st * P:(st + 1) * P], uv[:, ct, 4 * hc:4 * hc + 4, :].rearrange("p h d -> p (h d)"),
                                    start=(ct == 0), stop=(ct == KC - 1))
                ins.then_inc(job_done, 1)
            for hp in range(NH // 2):
                b = bank_for(JOB["k"] + hp)
                for e in range(2):
                    for ct in range(KC):
                        ins = pe.matmul(b[:, e * T:(e + 1) * T], uk[:, ct, 2 * hp + e, :], ckvT[:, ct, :],
                                        start=(ct == 0), stop=(ct == KC - 1))
                ins.then_inc(job_done, 1)

            def attend(layer):
                number, order = head_jobs(layer), heads(layer)
                before = len(heads(0)) * layer
                mkT, mv = ((mk0T, mv0), (mk1T, mv1))[layer]
                for s in range(len(order) + 2):
                    if s < len(order):
                        is_self, h = order[s]
                        q, k = (qT, kT) if is_self else (qmemT, mkT)
                        needed = (JOB[f"q{h // KPC}"] + h % KPC, JOB["k"] + h // 2) if is_self else (JOB[f"qmem{layer}"] + h, JOB[f"mk{layer}"] + h)
                        for j in needed:
                            wait_emptied(pe, j)
                        j = number["logits", s]
                        b = bank_for(j)
                        for qb in range(TT):
                            ins = pe.matmul(b[:, qb * T:(qb + 1) * T], q[:, h, qb * P:(qb + 1) * P], k[:, h, :], start=True, stop=True)
                        ins.then_inc(job_done, 1)
                    if 0 <= s - 1 < len(order):
                        b = bank_for(number["probs", s - 1])
                        pe.wait_ge(p_ready, before + s)
                        for st in range(TT):
                            for qb in range(TT):
                                ins = pe.transpose(b[:, st * T + qb * P:st * T + (qb + 1) * P],
                                                   lg[:, (s - 1) % 2, qb, st * P:(st + 1) * P], ident[:, :])
                        ins.then_inc(job_done, 1)
                    if 0 <= s - 2:
                        is_self, h = order[s - 2]
                        b = bank_for(number["output", s - 2])
                        wait_emptied(pe, number["probs", s - 2])
                        vals = v if is_self else mv
                        for st in range(TT):
                            ins = pe.matmul(b[:, 0:T], vals[:, st, h * HD:(h + 1) * HD], pT[:, s % 2, st, :],
                                            start=(st == 0), stop=(st == TT - 1))
                        ins.then_inc(job_done, 1)
                for s in range(len(order)):
                    wait_emptied(pe, number["output", s])

            def product_loop(name, hi, lo, per):
                c0, t0 = CHUNK[name], TILE[name]
                with pe.Fori(0, D // NW // 2) as i:
                    for half in range(2):
                        pe.wait_ge(taken[half], i + (c0 // 2))
                        for n in range(per):
                            products(t0 + half * per + n, n, hi, lo, half, per, i * (2 * per))

            def ffn(layer):
                t0, c0, job0 = TILE[f"ffn{layer}"], CHUNK[f"ffn{layer}"], JOB[f"hid{layer}"]

                def hidden_of(i):
                    pe.wait_ge(taken[1], i + (c0 // 2 + 1))
                    for k in range(KPC):
                        j = job0 + k
                        pe.wait_ge(emptied[j % NBANK], i + j // NBANK)
                        for tt in range(TT):
                            ins = pe.transpose(bank[j % NBANK][:, tt * P:(tt + 1) * P], stage[:, tt, k * P:(k + 1) * P], ident[:, :])
                        ins.then_inc(job_done, 1)

                wait_taken(pe, c0 - 1)
                chunk(c0, h_hi, h_lo, CT_D, fill_hooks(f"f{layer}", xres))
                chunk(c0 + 1, h_hi, h_lo, CT_D)
                with pe.Fori(1, FFN_IT) as i:
                    for half in range(2):
                        pe.wait_ge(taken[half], i + (c0 // 2))
                        for n in range(CT_D):
                            if half == 0 and n == 1:
                                hidden_of(i - 1)
                            products(t0 + half * CT_D + n, n, h_hi, h_lo, half, CT_D, i * (2 * CT_D))
                hidden_of(FFN_IT - 1)
                for k in range(KPC):
                    pe.wait_ge(emptied[(job0 + k) % NBANK], FFN_IT + (job0 + k) // NBANK)

            attend(0)
            product_loop("out0", mix_hi, mix_lo, CT_D)
            ffn(0)
            product_loop("down0", hid_hi, hid_lo, CT_F)

            c = CHUNK["in1"]
            wait_taken(pe, c - 2)
            wait_taken(pe, c - 1)
            chunk(c, h_hi, h_lo, CT_D, fill_hooks("h1", xres))
            chunk(c + 1, h_hi, h_lo, CT_D)

            def pooled(name, k0, number, u_chunk):
                def run():
                    wait_taken(pe, u_chunk)
                    pe.wait_ge(bands_ready, 2 * NG)
                    for n in range(number):
                        ct, b = k0 + n, bank_for(JOB[name] + n)
                        g = ct // KG
                        pe.matmul(b[:, 0:T], u1[:, 0, ct * P:(ct + 1) * P], bandA[:, g, :], start=True, stop=False)
                        pe.matmul(b[:, P:T], u1[:, 1, ct * P:(ct + 1) * P], bandC[:, g, :], start=False, stop=True).then_inc(job_done, 1)
                return run

            def grouped(name, g0, number):
                def run():
                    pe.wait_ge(wg_in, 16 * NG)
                    for g in range(g0, g0 + number):
                        for ct in range(KG * g, KG * (g + 1)):
                            wait_emptied(pe, JOB["pool01"] + ct if ct < 2 * KPC else JOB["pool2"] + ct - 2 * KPC)
                        for dt in range(KG):
                            b = bank_for(JOB[name] + (g - g0) * KG + dt)
                            for ct in range(KG):
                                ins = pe.matmul(b[:, 0:T], wg[:, g, ct, dt * P:(dt + 1) * P], yT[:, KG * g + ct, :],
                                                start=(ct == 0), stop=(ct == KG - 1))
                            ins.then_inc(job_done, 1)
                return run

            chunk(c + 2, h_hi, h_lo, CT_D, {4: pooled("pool01", 0, 2 * KPC, c + 1), 6: grouped("group0", 0, 1)})
            chunk(c + 3, h_hi, h_lo, CT_D, {4: pooled("pool2", 2 * KPC, KPC, c + 2)})
            grouped("group123", 1, 3)()
            wait_taken(pe, c + 3)
            transposes("qmem1", u1[:, :, PW:D], 0, MH)
            attend(1)
            product_loop("out1", mix_hi, mix_lo, CT_D)
            ffn(1)
            product_loop("down1", hid_hi, hid_lo, CT_F)


INPUTS = ["x", "mem", "mixer_norm", "ffn_norm", "final_norm", "mem_norm", "w_mem_kv", "w_out", "w_gate", "w_up", "w_down",
          "w_in_attn", "q_norm", "kv_norm", "w_uq", "w_uk", "w_uv", "w_idx_uq", "idx_k_norm", "idx_k_bias",
          "w_in_pool", "w_pool_group", "pool_scale"]


def kernel(**inputs):
    import numpy as np
    import concourse.bacc as bacc
    from concourse.bass_utils import run_bass_kernel_spmd

    nc = bacc.Bacc("TRN2", target_bir_lowering=False, num_devices=1)
    arrays, args = {}, []
    for name in INPUTS:
        a = np.ascontiguousarray(inputs[name])
        arrays[f"in_{name}"] = a
        args.append(nc.dram_tensor(f"in_{name}", a.shape, mybir.dt.from_np(a.dtype), kind="ExternalInput").ap())
    y = nc.dram_tensor("y", arrays["in_x"].shape, F32, kind="ExternalOutput").ap()
    trunk(nc, *args, y)
    result = run_bass_kernel_spmd(nc, [arrays], core_ids=[0])
    return result.results[0]["y"]
```

```python
from contextlib import ExitStack

import concourse.bass as bass
from concourse import mybir

F32 = mybir.dt.float32
F32R = mybir.dt.float32r
ACT = mybir.ActivationFunctionType
ALU = mybir.AluOpType
AX = mybir.AxisListType

P = 128
NW = 512
RING = 4
AHEAD = 3
NBANK = 4
EPS = 1e-6
LAG_P, LAG_O = 2, 3
SLOTS = LAG_P + 1
KEYS_LEAD = 2
MASKED = -1.0e30
NONCAUSAL = -1.0e38
TAKEN = -3.0e38
TAKEN_BELOW = -2.0e38


def trunk(nc, x, mem, mixer_norm, ffn_norm, final_norm, mem_norm, w_mem_kv, w_out, w_gate, w_up, w_down,
          w_in_attn, q_norm, kv_norm, w_uq, w_uk, w_uv, w_idx_uq, idx_k_norm, idx_k_bias,
          w_in_pool, w_pool_group, pool_scale, out):
    _, T, D = x.shape
    TT = T // P
    KD = D // P
    DFF = w_gate.shape[2]
    KF = DFF // P
    LAYERS = w_out.shape[0]
    NH, KVL, HD = w_uk.shape[1:]
    QL = q_norm.shape[1]
    KQ, KC = QL // P, KVL // P
    ID = idx_k_norm.shape[1]
    IH = w_idx_uq.shape[2] // ID
    MW = w_mem_kv.shape[2] // 2
    MH = MW // HD
    PW = pool_scale.shape[1]
    NG, PG = w_pool_group.shape[1], w_pool_group.shape[2]
    KG = PG // P
    TOPK = min(256, T // 4)
    ATTN_IN = w_in_attn.shape[2]
    C_KV, C_KI, C_WI, C_QM = QL, QL + KVL, QL + KVL + ID, QL + KVL + ID + IH
    SCALE = HD ** -0.5
    assert TT == 2 and HD == P and MW == NW and QL == NW and 2 * ID == P and T == 2 * P and LAYERS == 2
    assert C_QM + MW == ATTN_IN
    FFN_IT = DFF // NW
    CT_D, CT_F, CT_Q = KD // 2, KF // 2, KQ // 2
    KPC = NW // P

    TILE, CHUNK = {}, {}
    LAST = []
    tiles = 0
    for name, chunks, per in (("mem0", 2, CT_D), ("mem1", 2, CT_D), ("in0", 3, CT_D), ("idx", 2, CT_Q), ("uq", 3, CT_Q),
                              ("out0", 4, CT_D), ("ffn0", 2 * FFN_IT, CT_D), ("down0", 4, CT_F), ("in1", 4, CT_D),
                              ("out1", 4, CT_D), ("ffn1", 2 * FFN_IT, CT_D), ("down1", 4, CT_F)):
        TILE[name], CHUNK[name] = tiles, len(LAST)
        for _ in range(chunks):
            tiles += per
            LAST.append(tiles - 1)
    TILES = tiles
    X_CHUNKS = {"out0": 0, "down0": 4, "out1": 8, "down1": 12}
    HEADS = {"mem0": [(False, h) for h in range(MH)], "self0": [(True, h) for h in range(NH)],
             "mem1": [(False, h) for h in range(MH)]}
    HEADS_BEFORE = {"mem0": 0, "self0": MH, "mem1": MH + NH}
    JOB, TR = {}, {}

    def add(name, count, split=False, first=0):
        for n in range(first, first + count):
            if split:
                TR[name, n] = len(TR)
            JOB[name, n] = len(JOB)

    def keys_before(s):
        return [hp for hp in range(NH // 2) if max(0, 2 * hp - KEYS_LEAD) == s]

    def add_step(group, s):
        for what, lag in (("logits", 0), ("probs", LAG_P), ("output", LAG_O)):
            if 0 <= s - lag < len(HEADS[group]):
                add(f"{what}_{group}", 1, what == "output", s - lag)

    add("memT", KD, True)
    add("mk0", MH)
    add("h0", KD, True)
    add("mk1", MH)
    add("cq", KQ, True)
    add("ckv", KC)
    add("kidx", 1)
    add("qmem0", MH)
    MEM_STEPS = MH + LAG_O
    add_step("mem0", 0)
    add("qidx0", KPC)
    add_step("mem0", 1)
    add_step("mem0", 2)
    add("qidx1", KPC)
    add_step("mem0", 3)
    add("q0", KPC)
    for s in range(4, MEM_STEPS):
        add_step("mem0", s)
    add("score", IH)
    add("q1", KPC)
    add("q2", KPC)
    add("v", TT * NH // 4)
    for s in range(NH + LAG_O):
        for hp in keys_before(s):
            add("k", 1, first=hp)
        add_step("self0", s)
    add("f0", KD, True)
    add("hid0", KPC * FFN_IT, True)
    add("h1", KD, True)
    add("qmem1", MH)
    for s in range(MEM_STEPS):
        add_step("mem1", s)
    add("pool", 2 * KPC)
    add("group", 2 * KG, True)
    add("pool", KPC, first=2 * KPC)
    add("group", 2 * KG, True, first=2 * KG)
    add("f1", KD, True)
    add("hid1", KPC * FFN_IT, True)

    def kt_of(is_self, h):
        return h if is_self else NH + h

    def spans(is_self):
        return ((0, P), (P, P + T)) if is_self else ((0, T), (T, 2 * T))

    SPAN = P + T
    IN1_ORDER = [3, 0, 1, 2]

    with ExitStack() as ctx:
        def sb(name, shape, dt=F32):
            return ctx.enter_context(nc.sbuf_tensor(name, shape, dt))

        def sem(name):
            return ctx.enter_context(nc.semaphore(name))

        xres = sb("xres", [P, TT, D])
        raw = sb("raw", [P, RING, 2, NW])
        whi = sb("whi", [P, RING, 2, NW], F32R)
        wlo = sb("wlo", [P, RING, 2, NW], F32R)
        stage = sb("stage", [P, TT, NW])
        mk1T = sb("mk1T", [P, MH, T])
        mv1 = sb("mv1", [P, TT, MW])
        ident = sb("ident", [P, P])
        GROWS = dict(mix=0, ffn=LAYERS * KD, q=2 * LAYERS * KD)
        GROWS["kv"] = GROWS["q"] + KQ
        GROWS["pool"] = GROWS["kv"] + KC
        GROWS["ki"] = GROWS["pool"] + PW // P
        GROWS["kb"] = GROWS["ki"] + 1
        NGR = GROWS["kb"] + 1
        assert NGR <= P
        grow = sb("grow", [NGR, P])
        gain = sb("gain", [P, NGR])
        grow_mem = sb("grow_mem", [KD, P])
        gain_mem = sb("gain_mem", [P, KD])
        ssq = sb("ssq", [P, 9, TT, 4])
        rstd = sb("rstd", [P, 9, TT])
        gsc = sb("gsc", [P, 4, TT])
        ksum = sb("ksum", [P, TT])
        kmean = sb("kmean", [P, TT])
        widx = sb("widx", [P, TT, IH])
        max8 = sb("max8", [P, TT, 8])
        lmax = sb("lmax", [P, SLOTS, TT])
        lsum = sb("lsum", [P, SLOTS, TT])
        linv = sb("linv", [P, SLOTS, TT])

        def gcol(name, k):
            return gain[:, GROWS[name] + k:GROWS[name] + k + 1]

        def place(off, name, shape, dt=F32):
            with ExitStack() as s:
                if off:
                    s.enter_context(nc.sbuf_tensor(f"pad_{name}", [P, off // 4], F32))
                return s.enter_context(nc.sbuf_tensor(name, shape, dt))

        KB = 1024
        H = 0
        h_hi = place(H, "h_hi", [P, KD, T], F32R)
        h_lo = place(H + 16 * KB, "h_lo", [P, KD, T], F32R)
        uk = place(H, "uk", [P, KC, NH, HD])
        uv = place(H + 12 * KB, "uv", [P, KC, NH, HD])
        kT = place(H + 12 * KB, "kT", [P, NH, T])
        qidxT = place(H + 24 * KB, "qidxT", [P, IH // 2, T])
        gfin = place(H, "gfin", [P, D])
        M = H + 32 * KB
        mix_hi = place(M, "mix_hi", [P, KD, T], F32R)
        mix_lo = place(M + 16 * KB, "mix_lo", [P, KD, T], F32R)
        acc = place(M, "acc", [P, SPAN])
        work = place(M + 2 * KB, "work", [P, SPAN])
        relus = place(M + 4 * KB, "relus", [P, 2, SPAN])
        kdup = place(M + 8 * KB, "kdup", [P, TT, 2, ID])
        m = M + 32 * KB
        lg = place(m, "lg", [P, SLOTS, TT * T])
        cq_hi = place(m, "cq_hi", [P, KQ, T], F32R)
        cq_lo = place(m + 4 * KB, "cq_lo", [P, KQ, T], F32R)
        qmemT = place(m + 8 * KB, "qmemT", [P, MH, T])
        m += 12 * KB
        proj = place(m, "proj", [P, TT, ATTN_IN])
        n = m + 11 * KB
        ckvT = place(n, "ckvT", [P, KC, T])
        kidxT = place(n + 2 * KB, "kidxT", [P, T])
        maskb = place(n + 3 * KB, "maskb", [P, SPAN])
        mk0T = place(n + 5 * KB, "mk0T", [P, MH, T])
        mv0 = place(n + 9 * KB, "mv0", [P, TT, MW])
        qT = place(n + 13 * KB, "qT", [P, NH, T])
        v = place(n + 25 * KB, "v", [P, TT, NH * HD])
        lg_mem = place(n + 25 * KB, "lg_mem", [P, SLOTS, TT * T])
        pT_mem = place(n + 31 * KB, "pT_mem", [P, 2, TT * T])
        memt = place(n + 13 * KB, "memt", [P, TT, D])
        u1 = place(m, "u1", [P, TT, D])
        yT = place(m + 16 * KB, "yT", [P, PW // P, T])
        wg = place(m + 28 * KB, "wg", [P, NG, KG, PG])
        bandA = place(m + 46 * KB, "bandA", [P, NG, T])
        bandC = place(m + 50 * KB, "bandC", [P, NG, P])
        rcnt = place(m + 52 * KB, "rcnt", [P, T])
        hid_hi = place(M, "hid_hi", [P, KF, T], F32R)
        hid_lo = place(M + KF * KB, "hid_lo", [P, KF, T], F32R)

        psum = ctx.enter_context(nc.psum_tensor("psum", [P, 4 + NBANK, NW], F32))
        bank = [psum[:, 4 + b, :] for b in range(NBANK)]

        raw_in = [sem(f"raw_in{s}") for s in range(RING)]
        hi_ready = sem("hi_ready")
        lo_ready = sem("lo_ready")
        tile_used = sem("tile_used")
        taken = [sem("takenA"), sem("takenB")]
        job_done = sem("job_done")
        emptied = [sem(f"emptied{b}") for b in range(NBANK)]
        tr_hi = sem("tr_hi")
        mem_in = [sem(f"mem_in{q}") for q in range(4)]
        x_in = [sem(f"x_in{q}") for q in range(4)]
        gain_mem_in = sem("gain_mem_in")
        gains_in = sem("gains_in")
        gains_T = sem("gains_T")
        gains_ready = sem("gains_ready")
        ukv_in = sem("ukv_in")
        wg_in = sem("wg_in")
        gfin_in = sem("gfin_in")
        ident_ready = sem("ident_ready")
        ssq_ready = sem("ssq_ready")
        rstd_ready = sem("rstd_ready")
        pool_seq = sem("pool_seq")
        dve_seq = sem("dve_seq")
        x_new = sem("x_new")
        cq_normed = sem("cq_normed")
        kidx_centred = sem("kidx_centred")
        kv_normed = sem("kv_normed")
        scored = sem("scored")
        causal = sem("causal")
        mask_raw = sem("mask_raw")
        lg_ready = sem("lg_ready")
        exp_done = sem("exp_done")
        p_ready = sem("p_ready")
        counts_ready = sem("counts_ready")
        rcnt_ready = sem("rcnt_ready")
        bands_ready = sem("bands_ready")
        x_gained = sem("x_gained")
        out_piece = [sem("out_piece0"), sem("out_piece1")]
        out_done = sem("out_done")

        MEM, X0, CQ, CKV, KIDX, F0, X1, F1, FIN = range(9)
        FFN_NORM = (F0, F1)
        GAIN_LOADS = 9

        def fp(ap):
            return ap.bitcast(F32)

        def wait_chunk(eng, c):
            eng.wait_ge(tile_used, LAST[c] + 1)

        def wait_taken(eng, c):
            eng.wait_ge(taken[c % 2], c // 2 + 1)

        def wait_emptied(eng, name, n=0):
            j = JOB[name, n]
            eng.wait_ge(emptied[j % NBANK], j // NBANK + 1)

        def wait_job(eng, name, n=0):
            eng.wait_ge(job_done, JOB[name, n] + 1)

        def bank_of(name, n=0):
            return bank[JOB[name, n] % NBANK]

        def emptied_by(name, n=0):
            return emptied[JOB[name, n] % NBANK]

        def first(c):
            return LAST[c - 1] + 1 if c else 0

        def chunk_width(c):
            return C_QM - QL if c == CHUNK["in0"] + 1 else NW

        def tile_width(t):
            c = CHUNK["in0"] + 1
            return C_QM - QL if first(c) <= t <= LAST[c] else NW

        LG = {"mem0": lg_mem, "self0": lg, "mem1": lg}
        PT = {"mem0": pT_mem, "self0": stage, "mem1": stage}

        rows = lambda ap: ap.rearrange("(k p) -> k p", p=P)

        block = ctx.enter_context(nc.Block())

        @block.sync
        def _(sp):
            def load_tokens(dst, src, q, loaded):
                cols = slice(q * NW, (q + 1) * NW)
                sp.dma_start(dst[:, :, cols], src.rearrange("b (t p) d -> p (b t) d", p=P)[:, :, cols]).then_inc(loaded[q], 16)

            def load(w, k, cols, t, more=0):
                if t >= RING:
                    sp.wait_ge(lo_ready, more + (t - RING + 1))
                src = w.rearrange("(k p) n -> p k n", p=P)[:, 2 * k:2 * k + 2, cols]
                sp.dma_start(raw[:, t % RING, :, 0:src.shape[2]], src).then_inc(raw_in[t % RING], 16)

            def product(name, w, per, starts):
                for n, c0 in enumerate(starts):
                    for k in range(per):
                        t = TILE[name] + n * per + k
                        load(w, k, slice(c0, c0 + tile_width(t)), t)

            def product_loop(name, w, per):
                with sp.Fori(0, D // NW // 2) as i:
                    for half in range(2):
                        for k in range(per):
                            load(w, k, bass.ds(i * (2 * NW) + half * NW, NW), TILE[name] + half * per + k, i * (2 * per))

            for k in range(2 * CT_D):
                if k < 4:
                    load_tokens(memt, mem, k, mem_in)
                elif k < 8:
                    load_tokens(xres, x, k - 4, x_in)
                load(w_mem_kv[0], k % CT_D, slice(k // CT_D * NW, (k // CT_D + 1) * NW), TILE["mem0"] + k)
            product("mem1", w_mem_kv[1], CT_D, (0, NW))
            product("in0", w_in_attn[0], CT_D, (0, C_KV, C_QM))
            product("idx", w_idx_uq[0], CT_Q, (0, NW))
            product("uq", w_uq[0], CT_Q, (0, NW, 2 * NW))
            for layer in range(LAYERS):
                if layer:
                    product("in1", w_in_pool[0], CT_D, [n * NW for n in IN1_ORDER])
                product_loop(f"out{layer}", w_out[layer], CT_D)
                with sp.Fori(0, FFN_IT) as i:
                    for half, w in ((0, w_gate), (1, w_up)):
                        for k in range(CT_D):
                            load(w[layer], k, bass.ds(i * NW, NW), TILE[f"ffn{layer}"] + half * CT_D + k, i * (2 * CT_D))
                product_loop(f"down{layer}", w_down[layer], CT_F)

            outv = out.rearrange("b (t p) d -> p (b t) d", p=P)
            for n in range(2):
                for tt in (1, 0):
                    sp.wait_ge(out_piece[tt], n + 1)
                    sp.dma_start(outv[:, tt, n * (D // 2):(n + 1) * (D // 2)],
                                 xres[:, tt, n * (D // 2):(n + 1) * (D // 2)]).then_inc(out_done, 16)
            sp.wait_ge(out_done, 16 * 2 * TT)

        @block.gpsimd
        def _(pool):
            seq = [0]

            def step(ins):
                seq[0] += 1
                ins.then_inc(pool_seq, 1)
                pool.wait_ge(pool_seq, seq[0])

            step(pool.memset(ident[:, :], 0.0))
            pool.affine_select(out=ident[:, :], in_=ident[:, :], compare_op=ALU.not_equal, fill=1.0, base=0,
                               pattern=[[-1, P]], channel_multiplier=1).then_inc(ident_ready, 1)
            step(pool.memset(gsc[:, 3, :], -0.5))
            for name, src, number in (("mix", mixer_norm.rearrange("l (k p) -> (l k) p", p=P), LAYERS * KD),
                                      ("ffn", ffn_norm.rearrange("l (k p) -> (l k) p", p=P), LAYERS * KD),
                                      ("q", rows(q_norm[0]), KQ), ("kv", rows(kv_norm[0]), KC),
                                      ("pool", rows(pool_scale[0]), PW // P)):
                pool.dma_start(grow[GROWS[name]:GROWS[name] + number, :], src).then_inc(gains_in, 16)
            for name, src in (("ki", idx_k_norm), ("kb", idx_k_bias)):
                for h in range(2):
                    pool.dma_start(grow[GROWS[name]:GROWS[name] + 1, h * ID:(h + 1) * ID], src).then_inc(gains_in, 16)

            def rstd_of(n, width, parts):
                s = ssq[:, n, :, :]
                if parts == 4:
                    step(pool.tensor_tensor(s[:, :, 0:2], s[:, :, 0:2], s[:, :, 2:4], ALU.add))
                    step(pool.tensor_tensor(s[:, :, 0:1], s[:, :, 0:1], s[:, :, 1:2], ALU.add))
                var, est, sq = gsc[:, 0, :], gsc[:, 1, :], gsc[:, 2, :]
                step(pool.tensor_scalar(var, s[:, :, 0], 1.0 / width, EPS, ALU.mult, ALU.add))
                step(pool.tensor_tensor(est, var, gsc[:, 3, :], ALU.pow))
                step(pool.tensor_tensor(sq, est, est, ALU.mult))
                step(pool.tensor_tensor(sq, sq, var, ALU.mult))
                step(pool.tensor_scalar(sq, sq, -0.5, 1.5, ALU.mult, ALU.add))
                pool.tensor_tensor(rstd[:, n, :], est, sq, ALU.mult).then_inc(rstd_ready, 1)
                pool.wait_ge(rstd_ready, n + 1)

            pool.wait_ge(ssq_ready, MEM + 1)
            rstd_of(MEM, D, 4)
            pool.wait_ge(ssq_ready, X0 + 1)
            rstd_of(X0, D, 4)
            pool.wait_ge(ssq_ready, CQ + 1)
            rstd_of(CQ, QL, 1)
            pool.wait_ge(ssq_ready, CKV + 1)
            rstd_of(CKV, KVL, 1)
            pool.wait_ge(ssq_ready, KIDX + 1)
            rstd_of(KIDX, ID, 1)
            pool.wait_ge(tile_used, TILE["idx"])
            for ct in range(KC):
                pool.dma_start(uk[:, ct, :, :], w_uk[0, :, ct * P:(ct + 1) * P, :].rearrange("h c d -> c h d")).then_inc(ukv_in, 16)
                pool.dma_start(uv[:, ct, :, :], w_uv[0, :, ct * P:(ct + 1) * P, :].rearrange("h c d -> c h d")).then_inc(ukv_in, 16)
            pool.wait_ge(scored, TT * IH)
            for qb, (a, b) in enumerate(spans(True)):
                pool.affine_select(out=work[:, a:b], in_=acc[:, a:b], compare_op=ALU.is_ge, fill=NONCAUSAL,
                                   base=qb * P, pattern=[[-1, b - a]], channel_multiplier=1).then_inc(causal, 1)
            for qb, (a, b) in enumerate(spans(True)):
                pool.wait_ge(mask_raw, qb + 1)
                pool.affine_select(out=maskb[:, a:b], in_=maskb[:, a:b], compare_op=ALU.is_ge, fill=MASKED,
                                   base=qb * P, pattern=[[-1, b - a]], channel_multiplier=1).then_inc(causal, 1)
            wait_taken(pool, CHUNK["out0"] + 3)
            rstd_of(F0, D, 4)
            pool.wait_ge(tile_used, TILE["in1"])
            for g in range(NG):
                pool.dma_start(wg[:, g, :, :], w_pool_group[0, g].rearrange("(k p) d -> p k d", p=P)).then_inc(wg_in, 16)
            wait_taken(pool, CHUNK["down0"] + 3)
            rstd_of(X1, D, 4)
            counts = bandA[:, 0, :].bitcast(mybir.dt.int32)
            step(pool.iota(counts, pattern=[[1, T]], base=1, channel_multiplier=0))
            pool.tensor_copy(rcnt[:, :], counts).then_inc(counts_ready, 1)
            pool.wait_ge(rcnt_ready, 1)
            for g in range(NG):
                win = 2 ** (g + 1)
                step(pool.tensor_scalar(bandA[:, g, :], rcnt[:, :], 1.0 / win, None, ALU.max))
                step(pool.memset(bandC[:, g, :], 1.0 / win))
                for band, width in ((bandA, T), (bandC, P)):
                    step(pool.affine_select(out=band[:, g, :], in_=band[:, g, :], compare_op=ALU.is_ge, fill=0.0,
                                            base=0, pattern=[[1, width]], channel_multiplier=-1))
                    step(pool.affine_select(out=band[:, g, :], in_=band[:, g, :], compare_op=ALU.is_ge, fill=0.0,
                                            base=win - 1, pattern=[[-1, width]], channel_multiplier=1))
                    pool.tensor_tensor(band[:, g, 0:P], band[:, g, 0:P], ident[:, :], ALU.subtract).then_inc(bands_ready, 1)
            wait_taken(pool, CHUNK["out1"] + 3)
            rstd_of(F1, D, 4)
            pool.wait_ge(tile_used, TILE["down1"])
            pool.dma_start(gfin[:, :], final_norm.partition_broadcast(P)).then_inc(gfin_in, 16)
            wait_taken(pool, CHUNK["down1"] + 3)
            rstd_of(FIN, D, 4)

        @block.scalar
        def _(act):
            def convert(t, more=0):
                s, w = t % RING, tile_width(t)
                act.wait_ge(raw_in[s], more * (16 // RING) + 16 * (t // RING + 1))
                if t >= RING:
                    act.wait_ge(tile_used, more + (t - RING + 1))
                act.activation(whi[:, s, :, 0:w], raw[:, s, :, 0:w], ACT.Copy).then_inc(hi_ready, 1)

            nxt = [0]

            def convert_until(end):
                while nxt[0] < min(end, TILES):
                    convert(nxt[0])
                    nxt[0] += 1

            def convert_for(c, n):
                convert_until(first(c) + n + AHEAD)

            def hi_of(name, n, dst, scale):
                wait_job(act, name, n)
                act.activation(dst, bank_of(name, n)[:, 0:T], ACT.Copy, scale=scale).then_inc(tr_hi, 1)

            def squares(src, junk, norm, part):
                for tt in range(TT):
                    ins = act.activation(junk(tt), src(tt), ACT.Square, accum_out=ssq[:, norm, tt, part])
                return ins

            def take(c, dst, c0, norm=None):
                w = chunk_width(c)
                wait_chunk(act, c)
                if norm is not None:
                    act.wait_ge(rstd_ready, norm + 1)
                for tt in range(TT):
                    ins = act.activation(dst[:, tt, c0:c0 + w], psum[:, 2 * (c % 2) + tt, 0:w], ACT.Copy,
                                         scale=1.0 if norm is None else rstd[:, norm, tt:tt + 1])
                ins.then_inc(taken[c % 2], 1)

            def pair(c, tt, a, b):
                return psum[:, 2 * (c % 2) + tt, a:b]

            act.dma_start(grow_mem[:, :], rows(mem_norm)).then_inc(gain_mem_in, 16)

            act.wait_ge(gains_ready, 1)
            for k in range(KD):
                if k == 2 or k % KPC == 0:
                    convert_until(k // 2 + (k > 2))
                hi_of("memT", k, mix_hi[:, k, :], gain_mem[:, k:k + 1])
            for q in range(4):
                convert_until(2 * AHEAD + 1 + q)
                ins = squares(lambda tt: memt[:, tt, q * NW:(q + 1) * NW], lambda tt: memt[:, tt, q * NW:(q + 1) * NW], MEM, slice(q, q + 1))
            ins.then_inc(ssq_ready, 1)
            c = CHUNK["mem0"]
            convert_until(LAST[c] + 1 + AHEAD)
            take(c, stage, 0, MEM)
            act.wait_ge(ssq_ready, MEM + 1)
            for q in range(4):
                convert_for(c + 1, q + 1)
                act.wait_ge(x_in[q], 16)
                ins = squares(lambda tt: xres[:, tt, q * NW:(q + 1) * NW], lambda tt: memt[:, tt, q * NW:(q + 1) * NW], X0, slice(q, q + 1))
            ins.then_inc(ssq_ready, 1)

            act.wait_ge(gains_ready, 2)

            def first_input(k0):
                for k in range(k0, k0 + KPC):
                    hi_of("h0", k, h_hi[:, k, :], gcol("mix", k))

            convert_for(c + 1, 6)
            first_input(0)
            convert_until(LAST[c + 1] + 1 + AHEAD)
            take(c + 1, mv0, 0, MEM)
            c = CHUNK["mem1"]
            convert_for(c, 3)
            first_input(4)
            convert_for(c, 5)
            first_input(8)
            convert_until(LAST[c] + 1 + AHEAD)
            wait_job(act, "mk0", MH - 1)
            take(c, stage, 0, MEM)
            convert_for(c + 1, 3)
            first_input(12)
            convert_until(LAST[c + 1] + 1 + AHEAD)
            take(c + 1, mv1, 0, MEM)

            c = CHUNK["in0"]
            convert_until(LAST[c] + 1 + AHEAD)
            wait_chunk(act, c)
            act.wait_ge(rstd_ready, X0 + 1)
            wait_job(act, "mk1", MH - 1)
            for tt in range(TT):
                ins = act.activation(stage[:, tt, 0:QL], pair(c, tt, 0, QL), ACT.Square, scale=rstd[:, X0, tt:tt + 1],
                                     accum_out=ssq[:, CQ, tt, 0:1])
            ins.then_inc(ssq_ready, 1)
            take(c, proj, 0, X0)
            c += 1
            convert_for(c, 6)
            for k in range(KQ):
                hi_of("cq", k, cq_hi[:, k, :], gcol("q", k))
            convert_until(LAST[c] + 1 + AHEAD)
            wait_chunk(act, c)
            act.wait_ge(ssq_ready, CQ + 1)
            for tt in range(TT):
                act.activation(stage[:, tt, 0:ID], pair(c, tt, C_KI - C_KV, C_WI - C_KV), ACT.Copy,
                               scale=rstd[:, X0, tt:tt + 1], accum_out=ksum[:, tt:tt + 1])
                ins = act.activation(stage[:, tt, ID:ID + KVL], pair(c, tt, 0, KVL), ACT.Square,
                                     scale=rstd[:, X0, tt:tt + 1], accum_out=ssq[:, CKV, tt, 0:1])
            ins.then_inc(ssq_ready, 1)
            take(c, proj, C_KV, X0)
            act.wait_ge(kidx_centred, TT)
            for tt in range(TT):
                ins = act.activation(kdup[:, tt, 1, :], kdup[:, tt, 0, :], ACT.Square, accum_out=ssq[:, KIDX, tt, 0:1])
            ins.then_inc(ssq_ready, 1)
            c += 1
            convert_for(c, 5)
            wait_job(act, "kidx")
            act.activation(kidxT[:, :], bank_of("kidx")[:, 0:T], ACT.Identity, scale=gcol("ki", 0),
                           bias=gcol("kb", 0)).then_inc(emptied_by("kidx"), 1)
            convert_until(LAST[c] + 1 + AHEAD)
            take(c, proj, C_QM, X0)
            def attend(group, s):
                order, lg, pT = HEADS[group], LG[group], PT[group]
                if 0 <= s - LAG_P < len(order):
                    n = s - LAG_P
                    width = spans(order[n][0])[-1][1]
                    wait_job(act, f"probs_{group}", n)
                    if n >= 2:
                        wait_job(act, f"output_{group}", n - 2)
                    act.activation(pT[:, n % 2, 0:width], bank_of(f"probs_{group}", n)[:, 0:width],
                                   ACT.Copy).then_inc(emptied_by(f"probs_{group}", n), 1)
                if 0 <= s - LAG_O:
                    n = s - LAG_O
                    hi_of(f"output_{group}", n, mix_hi[:, kt_of(*order[n]), :], 1.0)
                if s < len(order):
                    slot = s % SLOTS
                    act.wait_ge(lg_ready, HEADS_BEFORE[group] + s + 1)
                    for qb, (a, b) in enumerate(spans(order[s][0])):
                        ins = act.activation(lg[:, slot, a:b], lg[:, slot, a:b], ACT.Exp, bias=lmax[:, slot, qb:qb + 1],
                                             accum_out=lsum[:, slot, qb:qb + 1])
                    ins.then_inc(exp_done, 1)

            c = CHUNK["idx"]
            convert_until(LAST[c] + 1 + AHEAD)
            act.wait_ge(ssq_ready, KIDX + 1)
            take(c, stage, 0)
            convert_until(LAST[c + 1] + 1 + AHEAD)
            take(c + 1, proj, 0)
            attend("mem0", 0)
            attend("mem0", 1)
            c = CHUNK["uq"]
            convert_until(LAST[c] + 1 + AHEAD)
            wait_job(act, "qidx0", KPC - 1)
            take(c, stage, 0)
            attend("mem0", 2)
            convert_until(LAST[c + 1] + 1 + AHEAD)
            wait_job(act, "qidx1", KPC - 1)
            take(c + 1, proj, 0)
            attend("mem0", 3)
            attend("mem0", 4)
            convert_until(LAST[c + 2] + 1 + AHEAD)
            wait_job(act, "q0", KPC - 1)
            take(c + 2, stage, 0)
            attend("mem0", 5)
            attend("mem0", 6)
            for h in range(IH):
                wait_job(act, "score", h)
                if h >= 2:
                    act.wait_ge(scored, TT * (h - 1))
                act.activation(relus[:, h % 2, :], bank_of("score", h)[:, 0:SPAN], ACT.Relu).then_inc(emptied_by("score", h), 1)
            for n in range(2):
                for k in range(KPC):
                    wait_job(act, f"q{n + 1}", k)
                    act.activation(qT[:, (n + 1) * KPC + k, :], bank_of(f"q{n + 1}", k)[:, 0:T],
                                   ACT.Copy).then_inc(emptied_by(f"q{n + 1}", k), 1)
            for j in range(TT * NH // 4):
                wait_job(act, "v", j)
                st, hc = j % TT, j // TT
                act.activation(v[:, st, hc * NW:(hc + 1) * NW], bank_of("v", j), ACT.Copy).then_inc(emptied_by("v", j), 1)
            for s in range(NH):
                for hp in keys_before(s):
                    wait_job(act, "k", hp)
                    act.activation(kT[:, 2 * hp:2 * hp + 2, :], bank_of("k", hp).rearrange("p (h s) -> p h s", h=2),
                                   ACT.Copy).then_inc(emptied_by("k", hp), 1)
                attend("self0", s)

            def residual(name, per, norm, next_input=None):
                c0 = CHUNK[name]
                for n in range(D // NW):
                    convert_until(LAST[c0 + n] + 1 + AHEAD)
                    if next_input:
                        for k in range(KPC * n, KPC * (n + 1)):
                            hi_of(next_input[0], k, h_hi[:, k, :], gcol(next_input[1], next_input[2] + k))
                    act.wait_ge(x_new, X_CHUNKS[name] + n + 1)
                    squares(lambda tt: xres[:, tt, n * NW:(n + 1) * NW], lambda tt: pair(c0 + n, tt, 0, NW), norm,
                            slice(n, n + 1)).then_inc(taken[n % 2], 1)

            def ffn(layer):
                t0, c0, job0, norm = TILE[f"ffn{layer}"], CHUNK[f"ffn{layer}"], JOB[f"hid{layer}", 0], FFN_NORM[layer]

                def silu(more):
                    act.wait_ge(tile_used, more + (LAST[c0] + 1))
                    act.wait_ge(rstd_ready, norm + 1)
                    for tt in range(TT):
                        ins = act.activation(stage[:, tt, :], pair(c0, tt, 0, NW), ACT.Silu, scale=rstd[:, norm, tt:tt + 1])
                    ins.then_inc(taken[0], 1)

                def hidden(kt):
                    for k in range(KPC):
                        j = job0 + k
                        act.wait_ge(job_done, kt + (j + 1))
                        act.activation(hid_hi[:, bass.ds(kt + k, 1), :].rearrange("p a t -> p (a t)"),
                                       bank[j % NBANK][:, 0:T], ACT.Copy).then_inc(tr_hi, 1)

                with act.Fori(0, FFN_IT) as i:
                    for k in range(CT_D):
                        convert(t0 + AHEAD + k, i * (2 * CT_D))
                    silu(i * (2 * CT_D))
                    for k in range(CT_D, 2 * CT_D):
                        convert(t0 + AHEAD + k, i * (2 * CT_D))
                    hidden(i * KPC)
                nxt[0] += 2 * CT_D * FFN_IT

            c = CHUNK["out0"]
            for n in range(LAG_O):
                convert_for(c, n + 1)
                attend("self0", NH + n)
            residual("out0", CT_D, F0, ("f0", "ffn", 0))
            ffn(0)
            residual("down0", CT_F, X1, ("h1", "mix", KD))

            c = CHUNK["in1"]

            def group(g):
                for n in range(g * KG, (g + 1) * KG):
                    hi_of("group", n, mix_hi[:, n, :], gcol("pool", n))

            def take_in1(n):
                convert_until(LAST[c + n] + 1 + AHEAD)
                take(c + n, u1, IN1_ORDER[n] * NW, X1)

            take_in1(0)
            take_in1(1)
            for s in range(MEM_STEPS):
                convert_for(c + 2, s + 1)
                attend("mem1", s)
            take_in1(2)
            convert_for(c + 3, 5)
            group(0)
            convert_for(c + 3, 6)
            group(1)
            take_in1(3)
            for g in (2, 3):
                convert_for(c + 4, g)
                group(g)
            residual("out1", CT_D, F1, ("f1", "ffn", KD))
            ffn(1)
            residual("down1", CT_F, FIN)
            act.wait_ge(x_gained, 4)
            act.wait_ge(rstd_ready, FIN + 1)
            for n in range(2):
                cols = xres[:, 0, n * (D // 2):(n + 1) * (D // 2)]
                act.activation(cols, cols, ACT.Copy, scale=rstd[:, FIN, 0:1]).then_inc(out_piece[0], 1)

        @block.vector
        def _(dve):
            seq = [0]

            def did(ins):
                seq[0] += 1
                ins.then_inc(dve_seq, 1)
                return seq[0]

            def convert(t, more=0):
                s, w = t % RING, tile_width(t)
                dve.wait_ge(hi_ready, more + (t + 1))
                dve.tensor_tensor(wlo[:, s, :, 0:w], raw[:, s, :, 0:w], fp(whi[:, s, :, 0:w]), ALU.subtract).then_inc(lo_ready, 1)

            nxt = [0]

            def convert_until(end):
                while nxt[0] < min(end, TILES):
                    convert(nxt[0])
                    nxt[0] += 1

            def convert_for(c, n):
                convert_until(first(c) + n + AHEAD)

            def lo_of(name, n, dst, hi, scale):
                dve.wait_ge(tr_hi, TR[name, n] + 1)
                dve.scalar_tensor_tensor(out=dst, in0=bank_of(name, n)[:, 0:T], scalar=scale, in1=fp(hi), op0=ALU.mult,
                                         op1=ALU.subtract).then_inc(emptied_by(name, n), 1)

            def copy_of(name, n, dst):
                wait_job(dve, name, n)
                dve.tensor_copy(dst, bank_of(name, n)[:, 0:T]).then_inc(emptied_by(name, n), 1)

            dve.wait_ge(gains_T, 1)
            dve.tensor_copy(gain_mem[:, :], psum[:, 3, 0:KD]).then_inc(gains_ready, 1)
            dve.wait_ge(gains_ready, 1)
            for k in range(KD):
                if k == 2 or k % KPC == 0:
                    convert_until(k // 2 + (k > 2))
                lo_of("memT", k, mix_lo[:, k, :], mix_hi[:, k, :], gain_mem[:, k:k + 1])
            dve.wait_ge(gains_T, 2)
            dve.tensor_copy(gain[:, :], psum[:, 3, 0:NGR]).then_inc(gains_ready, 1)
            dve.wait_ge(gains_ready, 2)

            def first_input(k0):
                for k in range(k0, k0 + KPC):
                    lo_of("h0", k, h_lo[:, k, :], h_hi[:, k, :], gcol("mix", k))

            def mem_keys(l, dst):
                convert_for(CHUNK[f"mem{l}"] + 1, 4)
                for h in range(MH):
                    copy_of(f"mk{l}", h, dst[:, h, :])

            c = CHUNK["mem0"]
            mem_keys(0, mk0T)
            convert_for(c + 1, 6)
            first_input(0)
            c = CHUNK["mem1"]
            convert_for(c, 3)
            first_input(4)
            convert_for(c, 5)
            first_input(8)
            convert_for(c + 1, 3)
            first_input(12)
            mem_keys(1, mk1T)

            c = CHUNK["in0"]
            convert_until(LAST[c] + 1 + 4)
            wait_taken(dve, c)
            dve.wait_ge(rstd_ready, CQ + 1)
            for tt in range(TT):
                dve.tensor_scalar(proj[:, tt, 0:QL], proj[:, tt, 0:QL], rstd[:, CQ, tt:tt + 1], None, ALU.mult).then_inc(cq_normed, 1)
            c += 1
            convert_for(c, 6)
            for k in range(KQ):
                lo_of("cq", k, cq_lo[:, k, :], cq_hi[:, k, :], gcol("q", k))
            convert_until(LAST[c] + 1 + AHEAD)
            wait_taken(dve, c)
            dve.wait_ge(dve_seq, did(dve.tensor_scalar(kmean[:, :], ksum[:, :], -1.0 / ID, None, ALU.mult)))
            for tt in range(TT):
                dve.tensor_scalar(kdup[:, tt, 0, :], proj[:, tt, C_KI:C_WI], kmean[:, tt:tt + 1], None, ALU.add).then_inc(kidx_centred, 1)
            dve.tensor_scalar(widx[:, :, :], proj[:, :, C_WI:C_QM], IH ** -0.5 * ID ** -0.5, None, ALU.mult)
            convert_until(LAST[c] + 1 + 4)
            dve.wait_ge(rstd_ready, CKV + 1)
            for tt in range(TT):
                dve.tensor_scalar(proj[:, tt, C_KV:C_KI], proj[:, tt, C_KV:C_KI], rstd[:, CKV, tt:tt + 1], None, ALU.mult).then_inc(kv_normed, 1)
            c += 1
            convert_for(c, 3)
            dve.wait_ge(rstd_ready, KIDX + 1)
            for tt in range(TT):
                dve.tensor_scalar(kdup[:, tt, 1, :], kdup[:, tt, 0, :], rstd[:, KIDX, tt:tt + 1], None, ALU.mult).then_inc(kv_normed, 1)
                dve.tensor_scalar(kdup[:, tt, 0, :], kdup[:, tt, 0, :], rstd[:, KIDX, tt:tt + 1], None, ALU.mult).then_inc(kv_normed, 1)
            convert_for(c, 5)
            for k in range(KC):
                wait_job(dve, "ckv", k)
                dve.tensor_scalar(ckvT[:, k, :], bank_of("ckv", k)[:, 0:T], gcol("kv", k), None, ALU.mult).then_inc(emptied_by("ckv", k), 1)

            def attend(group, s):
                order, lg = HEADS[group], LG[group]
                if s < len(order):
                    is_self, h = order[s]
                    slot, both = s % SLOTS, spans(is_self)
                    width = both[-1][1]
                    if is_self and h == 0:
                        dve.wait_ge(causal, 2 * TT)
                    wait_job(dve, f"logits_{group}", s)
                    if s >= SLOTS:
                        wait_job(dve, f"probs_{group}", s - SLOTS)
                    src, dst = bank_of(f"logits_{group}", s)[:, 0:width], lg[:, slot, 0:width]
                    if is_self:
                        ins = dve.scalar_tensor_tensor(out=dst, in0=src, scalar=SCALE, in1=maskb[:, :], op0=ALU.mult, op1=ALU.add)
                    else:
                        ins = dve.tensor_scalar(dst, src, SCALE, None, ALU.mult)
                    ins.then_inc(emptied_by(f"logits_{group}", s), 1)
                    wait_emptied(dve, f"logits_{group}", s)
                    for qb, (a, b) in enumerate(both):
                        ins = dve.tensor_reduce(out=lmax[:, slot, qb:qb + 1], in_=lg[:, slot, a:b], axis=AX.X, op=ALU.max, negate=True)
                    ins.then_inc(lg_ready, 1)
                if 0 <= s - 1 < len(order):
                    slot = (s - 1) % SLOTS
                    dve.wait_ge(exp_done, HEADS_BEFORE[group] + s)
                    dve.wait_ge(dve_seq, did(dve.reciprocal(linv[:, slot, :], lsum[:, slot, :])))
                    for qb, (a, b) in enumerate(spans(order[s - 1][0])):
                        ins = dve.tensor_scalar(lg[:, slot, a:b], lg[:, slot, a:b], linv[:, slot, qb:qb + 1], None, ALU.mult)
                    ins.then_inc(p_ready, 1)
                if 0 <= s - LAG_O:
                    n = s - LAG_O
                    kt = kt_of(*order[n])
                    lo_of(f"output_{group}", n, mix_lo[:, kt, :], mix_hi[:, kt, :], 1.0)

            c = CHUNK["idx"]
            convert_until(LAST[c] + 1 + AHEAD)
            for h in range(MH):
                copy_of("qmem0", h, qmemT[:, h, :])
            convert_until(LAST[c + 1] + 1 + AHEAD)
            attend("mem0", 0)
            for k in range(KPC):
                copy_of("qidx0", k, qidxT[:, k, :])
            attend("mem0", 1)
            c = CHUNK["uq"]
            convert_until(LAST[c] + 1 + AHEAD)
            attend("mem0", 2)
            for k in range(KPC):
                copy_of("qidx1", k, qidxT[:, KPC + k, :])
            convert_until(LAST[c + 1] + 1 + AHEAD)
            attend("mem0", 3)
            for k in range(KPC):
                copy_of("q0", k, qT[:, k, :])
            attend("mem0", 4)
            convert_until(LAST[c + 2] + 1 + AHEAD)
            attend("mem0", 5)
            attend("mem0", 6)
            for h in range(IH):
                wait_emptied(dve, "score", h)
                for qb, (a, b) in enumerate(spans(True)):
                    w = widx[:, qb, h:h + 1]
                    if h == 0:
                        dve.tensor_scalar(acc[:, a:b], relus[:, 0, a:b], w, None, ALU.mult).then_inc(scored, 1)
                    else:
                        dve.wait_ge(scored, TT * (h - 1) + qb + 1)
                        dve.scalar_tensor_tensor(out=acc[:, a:b], in0=relus[:, h % 2, a:b], scalar=w, in1=acc[:, a:b],
                                                 op0=ALU.mult, op1=ALU.add).then_inc(scored, 1)
            written = [None, None]
            for r in range(TOPK // 8):
                best = []
                for qb, (a, b) in enumerate(spans(True)):
                    if r == 0:
                        dve.wait_ge(causal, qb + 1)
                    else:
                        dve.wait_ge(dve_seq, written[qb])
                    best.append(did(dve.max(out=max8[:, qb, :], in_=work[:, a:b])))
                for qb, (a, b) in enumerate(spans(True)):
                    dve.wait_ge(dve_seq, best[qb])
                    written[qb] = did(dve.match_replace(out=work[:, a:b], in_to_replace=max8[:, qb, :], in_values=work[:, a:b],
                                                        imm_value=TAKEN))
            for qb, (a, b) in enumerate(spans(True)):
                dve.wait_ge(dve_seq, written[qb])
                dve.tensor_scalar(maskb[:, a:b], work[:, a:b], TAKEN_BELOW, MASKED, ALU.is_gt, ALU.mult).then_inc(mask_raw, 1)
            for s in range(NH):
                attend("self0", s)

            def final_gain(n):
                wait_taken(dve, CHUNK["down1"] + n)
                dve.wait_ge(gfin_in, 16)
                for tt in range(TT):
                    cols = xres[:, tt, n * NW:(n + 1) * NW]
                    ins = dve.tensor_tensor(cols, cols, gfin[:, n * NW:(n + 1) * NW], ALU.mult)
                ins.then_inc(x_gained, 1)

            def residual(name, next_input=None):
                c0 = CHUNK[name]
                for n in range(D // NW):
                    convert_until(LAST[c0 + n] + 1 + AHEAD)
                    wait_chunk(dve, c0 + n)
                    cols = xres[:, :, n * NW:(n + 1) * NW]
                    dve.tensor_tensor(cols, cols, psum[:, 2 * (n % 2):2 * (n % 2) + 2, :], ALU.add).then_inc(x_new, 1)
                    if not next_input and n:
                        final_gain(n - 1)
                    if next_input:
                        for k in range(KPC * n, KPC * (n + 1)):
                            lo_of(next_input[0], k, h_lo[:, k, :], h_hi[:, k, :], gcol(next_input[1], next_input[2] + k))

            def ffn(layer):
                t0, c0, job0, norm = TILE[f"ffn{layer}"], CHUNK[f"ffn{layer}"], JOB[f"hid{layer}", 0], FFN_NORM[layer]
                tr0 = TR[f"hid{layer}", 0]
                flat = lambda h, kt: h[:, bass.ds(kt, 1), :].rearrange("p a t -> p (a t)")
                with dve.Fori(0, FFN_IT) as i:
                    for k in range(2 * CT_D):
                        convert(t0 + AHEAD + k, i * (2 * CT_D))
                    dve.wait_ge(tile_used, i * (2 * CT_D) + (LAST[c0 + 1] + 1))
                    dve.wait_ge(taken[0], i + (c0 // 2 + 1))
                    dve.wait_ge(rstd_ready, norm + 1)
                    for tt in range(TT):
                        ins = dve.scalar_tensor_tensor(out=stage[:, tt, :], in0=psum[:, 2 + tt, :], scalar=rstd[:, norm, tt:tt + 1],
                                                       in1=stage[:, tt, :], op0=ALU.mult, op1=ALU.mult)
                    ins.then_inc(taken[1], 1)
                    for k in range(KPC):
                        j, kt = job0 + k, i * KPC + k
                        dve.wait_ge(tr_hi, i * KPC + (tr0 + k + 1))
                        dve.tensor_tensor(flat(hid_lo, kt), bank[j % NBANK][:, 0:T], fp(flat(hid_hi, kt)),
                                          ALU.subtract).then_inc(emptied[j % NBANK], 1)
                nxt[0] += 2 * CT_D * FFN_IT

            c = CHUNK["out0"]
            for n in range(LAG_O):
                convert_for(c, n + 1)
                attend("self0", NH + n)
            residual("out0", ("f0", "ffn", 0))
            ffn(0)
            residual("down0", ("h1", "mix", KD))

            c = CHUNK["in1"]

            def group(g):
                for n in range(g * KG, (g + 1) * KG):
                    lo_of("group", n, mix_lo[:, n, :], mix_hi[:, n, :], gcol("pool", n))

            convert_for(c + 1, 3)
            for h in range(MH):
                copy_of("qmem1", h, qmemT[:, h, :])
            dve.wait_ge(counts_ready, 1)
            dve.reciprocal(rcnt[:, :], rcnt[:, :]).then_inc(rcnt_ready, 1)
            for s in range(MEM_STEPS):
                convert_for(c + 2, s + 1)
                attend("mem1", s)
            convert_for(c + 3, 2)
            for k in range(2 * KPC):
                copy_of("pool", k, yT[:, k, :])
            convert_for(c + 3, 5)
            group(0)
            convert_for(c + 3, 6)
            group(1)
            convert_for(c + 4, 1)
            for k in range(2 * KPC, 3 * KPC):
                copy_of("pool", k, yT[:, k, :])
            for g in (2, 3):
                convert_for(c + 4, g)
                group(g)
            residual("out1", ("f1", "ffn", KD))
            ffn(1)
            residual("down1")

            final_gain(3)
            dve.wait_ge(rstd_ready, FIN + 1)
            dve.wait_ge(x_gained, 4)
            for n in range(2):
                cols = xres[:, 1, n * (D // 2):(n + 1) * (D // 2)]
                dve.tensor_scalar(cols, cols, rstd[:, FIN, 1:2], None, ALU.mult).then_inc(out_piece[1], 1)

        @block.tensor
        def _(pe):
            def products(t, n, hi, lo, p, tiles_in_chunk, more=0):
                w = tile_width(t)
                pe.wait_ge(lo_ready, more + (t + 1))
                for k in (2 * n, 2 * n + 1):
                    for tt in range(TT):
                        for a, b in ((hi, whi), (hi, wlo), (lo, whi)):
                            ins = pe.matmul(psum[:, 2 * p + tt, 0:w], a[:, k, tt * P:(tt + 1) * P], b[:, t % RING, k % 2, 0:w],
                                            start=(k == 0 and a is hi and b is whi),
                                            stop=(k == 2 * tiles_in_chunk - 1 and a is lo))
                ins.then_inc(tile_used, 1)

            def chunk(c, hi, lo, before={}, needs={}):
                per = LAST[c] - first(c) + 1
                if c >= 2:
                    wait_taken(pe, c - 2)
                for n in range(per):
                    if n in before:
                        before[n]()
                    for name, j in needs.get(n, ()):
                        wait_emptied(pe, name, j)
                    products(first(c) + n, n, hi, lo, c % 2, per)

            def bank_for(name, n=0):
                j = JOB[name, n]
                if j >= NBANK:
                    pe.wait_ge(emptied[j % NBANK], j // NBANK)
                return bank[j % NBANK]

            def transposes(name, src, k0, number, n0=0):
                for n in range(number):
                    b = bank_for(name, n0 + n)
                    for tt in range(TT):
                        ins = pe.transpose(b[:, tt * P:(tt + 1) * P], src[:, tt, (k0 + n) * P:(k0 + n + 1) * P], ident[:, :])
                    ins.then_inc(job_done, 1)

            def k_jobs(name, tiles):
                return {n: [(name, 2 * n), (name, 2 * n + 1)] for n in tiles}

            def memory(k0):
                def run():
                    pe.wait_ge(mem_in[k0 // KPC], 16)
                    transposes("memT", memt, k0, KPC, k0)
                    if k0 == 0:
                        pe.wait_ge(gain_mem_in, 16)
                        pe.transpose(psum[:, 3, 0:KD], grow_mem[:, :], ident[0:KD, 0:KD]).then_inc(gains_T, 1)
                    if k0 == KD - KPC:
                        pe.wait_ge(gains_in, 16 * GAIN_LOADS)
                        pe.wait_ge(gains_ready, 1)
                        pe.transpose(psum[:, 3, 0:NGR], grow[:, :], ident[0:NGR, 0:NGR]).then_inc(gains_T, 1)
                return run

            pe.wait_ge(ident_ready, 1)
            c = CHUNK["mem0"]
            chunk(c, mix_hi, mix_lo, {0: memory(0), 1: memory(4), 3: memory(8), 5: memory(12)}, k_jobs("memT", range(CT_D)))
            pe.wait_ge(gains_ready, 2)

            def mem_keys(l):
                def run():
                    wait_taken(pe, CHUNK[f"mem{l}"])
                    transposes(f"mk{l}", stage, 0, MH)
                return run

            def first_input(k0):
                def run():
                    pe.wait_ge(x_in[k0 // KPC], 16)
                    transposes("h0", xres, k0, KPC, k0)
                return run

            chunk(c + 1, mix_hi, mix_lo, {4: mem_keys(0), 6: first_input(0)})
            chunk(c + 2, mix_hi, mix_lo, {3: first_input(4), 5: first_input(8)})
            chunk(c + 3, mix_hi, mix_lo, {3: first_input(12), 4: mem_keys(1)})

            c = CHUNK["in0"]
            chunk(c, h_hi, h_lo, {}, k_jobs("h0", range(CT_D)))

            def latent_queries():
                pe.wait_ge(cq_normed, TT)
                transposes("cq", proj, 0, KQ)

            def latent_keys():
                pe.wait_ge(kv_normed, TT)
                transposes("ckv", proj[:, :, C_KV:C_KI], 0, KC)
                pe.wait_ge(kv_normed, 3 * TT)
                transposes("kidx", kdup[:, :, :, :].rearrange("p t a d -> p t (a d)"), 0, 1)

            chunk(c + 1, h_hi, h_lo, {6: latent_queries})
            chunk(c + 2, h_hi, h_lo, {5: latent_keys})

            def attend(group, s):
                order, lg, pT = HEADS[group], LG[group], PT[group]
                layer = int(group[-1])
                mkT, mv = ((mk0T, mv0), (mk1T, mv1))[layer]
                if s < len(order):
                    is_self, h = order[s]
                    q, k = (qT, kT) if is_self else (qmemT, mkT)
                    if is_self:
                        wait_emptied(pe, f"q{h // KPC}", h % KPC)
                        wait_emptied(pe, "k", h // 2)
                    else:
                        wait_emptied(pe, f"qmem{layer}", h)
                        wait_emptied(pe, f"mk{layer}", h)
                    b = bank_for(f"logits_{group}", s)
                    for qb, (a, e) in enumerate(spans(is_self)):
                        ins = pe.matmul(b[:, a:e], q[:, h, qb * P:(qb + 1) * P], k[:, h, 0:e - a], start=True, stop=True)
                    ins.then_inc(job_done, 1)
                if 0 <= s - LAG_P < len(order):
                    n = s - LAG_P
                    b = bank_for(f"probs_{group}", n)
                    pe.wait_ge(p_ready, HEADS_BEFORE[group] + n + 1)
                    at = 0
                    for st in range(TT):
                        for a, e in spans(order[n][0]):
                            if a + st * P < e:
                                ins = pe.transpose(b[:, at:at + P], lg[:, n % SLOTS, a + st * P:a + (st + 1) * P], ident[:, :])
                                at += P
                    ins.then_inc(job_done, 1)
                if 0 <= s - LAG_O:
                    n = s - LAG_O
                    is_self, h = order[n]
                    b = bank_for(f"output_{group}", n)
                    wait_emptied(pe, f"probs_{group}", n)
                    vals, q0 = (v, P) if is_self else (mv, 0)
                    pe.matmul(b[:, 0:T], vals[:, 0, h * HD:(h + 1) * HD], pT[:, n % 2, 0:T], start=True, stop=False)
                    pe.matmul(b[:, q0:T], vals[:, 1, h * HD:(h + 1) * HD], pT[:, n % 2, T:2 * T - q0], start=False,
                              stop=True).then_inc(job_done, 1)

            c = CHUNK["idx"]
            chunk(c, cq_hi, cq_lo, {}, {0: [("cq", k) for k in range(KQ)]})
            wait_taken(pe, CHUNK["in0"] + 2)
            transposes("qmem0", proj[:, :, C_QM:ATTN_IN], 0, MH)
            chunk(c + 1, cq_hi, cq_lo)
            wait_taken(pe, CHUNK["mem0"] + 1)
            attend("mem0", 0)
            wait_taken(pe, c)
            transposes("qidx0", stage, 0, KPC)
            attend("mem0", 1)
            c = CHUNK["uq"]
            chunk(c, cq_hi, cq_lo)
            attend("mem0", 2)
            wait_taken(pe, c - 1)
            transposes("qidx1", proj, 0, KPC)
            chunk(c + 1, cq_hi, cq_lo)
            attend("mem0", 3)
            wait_taken(pe, c)
            transposes("q0", stage, 0, KPC)
            attend("mem0", 4)
            chunk(c + 2, cq_hi, cq_lo)
            attend("mem0", 5)
            attend("mem0", 6)
            wait_emptied(pe, "kidx")
            for h in range(IH):
                wait_emptied(pe, f"qidx{h // 2 // KPC}", h // 2 % KPC)
                b, r = bank_for("score", h), ID * (h % 2)
                for qb, (a, e) in enumerate(spans(True)):
                    ins = pe.matmul(b[:, a:e], qidxT[r:r + ID, h // 2, qb * P:(qb + 1) * P], kidxT[r:r + ID, 0:e - a],
                                    start=True, stop=True)
                ins.then_inc(job_done, 1)
            wait_taken(pe, c + 1)
            transposes("q1", proj, 0, KPC)
            wait_taken(pe, c + 2)
            transposes("q2", stage, 0, KPC)
            pe.wait_ge(ukv_in, 16 * 2 * KC)
            for k in range(KC):
                wait_emptied(pe, "ckv", k)
            for j in range(TT * NH // 4):
                b, st, hc = bank_for("v", j), j % TT, j // TT
                for ct in range(KC):
                    ins = pe.matmul(b, ckvT[:, ct, st * P:(st + 1) * P], uv[:, ct, 4 * hc:4 * hc + 4, :].rearrange("p h d -> p (h d)"),
                                    start=(ct == 0), stop=(ct == KC - 1))
                ins.then_inc(job_done, 1)
            for s in range(NH):
                for hp in keys_before(s):
                    b = bank_for("k", hp)
                    for e in range(2):
                        for ct in range(KC):
                            ins = pe.matmul(b[:, e * T:(e + 1) * T], uk[:, ct, 2 * hp + e, :], ckvT[:, ct, :],
                                            start=(ct == 0), stop=(ct == KC - 1))
                    ins.then_inc(job_done, 1)
                attend("self0", s)

            def new_input(name, x_chunks, n):
                def run():
                    pe.wait_ge(x_new, x_chunks + n + 1)
                    transposes(name, xres, KPC * n, KPC, KPC * n)
                return run

            def hidden_of(layer, i):
                c0, job0 = CHUNK[f"ffn{layer}"], JOB[f"hid{layer}", 0]
                pe.wait_ge(taken[1], i + (c0 // 2 + 1))
                for k in range(KPC):
                    j = job0 + k
                    pe.wait_ge(emptied[j % NBANK], i + j // NBANK)
                    for tt in range(TT):
                        ins = pe.transpose(bank[j % NBANK][:, tt * P:(tt + 1) * P], stage[:, tt, k * P:(k + 1) * P], ident[:, :])
                    ins.then_inc(job_done, 1)

            def ffn(layer):
                t0, c0, name = TILE[f"ffn{layer}"], CHUNK[f"ffn{layer}"], f"f{layer}"
                chunk(c0, h_hi, h_lo, {1: new_input(name, X_CHUNKS[f"out{layer}"], 3)}, k_jobs(name, range(CT_D)))
                chunk(c0 + 1, h_hi, h_lo)
                with pe.Fori(1, FFN_IT) as i:
                    for half in range(2):
                        pe.wait_ge(taken[half], i + (c0 // 2))
                        for n in range(CT_D):
                            if half == 0 and n == 1:
                                hidden_of(layer, i - 1)
                            products(t0 + half * CT_D + n, n, h_hi, h_lo, half, CT_D, i * (2 * CT_D))

            def out_product(layer, before, needs):
                c, name, xc = CHUNK[f"out{layer}"], f"f{layer}", X_CHUNKS[f"out{layer}"]
                chunk(c, mix_hi, mix_lo, before, needs)
                for n in range(1, 4):
                    chunk(c + n, mix_hi, mix_lo, {1: new_input(name, xc, n - 1)})

            def down_product(layer, name):
                c, xc, hid = CHUNK[f"down{layer}"], X_CHUNKS[f"down{layer}"], f"hid{layer}"
                chunk(c, hid_hi, hid_lo, {1: lambda: hidden_of(layer, FFN_IT - 1)}, k_jobs(hid, range(CT_F)))
                for n in range(1, 4):
                    chunk(c + n, hid_hi, hid_lo, {1: new_input(name, xc, n - 1)} if name else {})

            out_product(0, {1 + n: lambda n=n: attend("self0", NH + n) for n in range(LAG_O)},
                        {n: [(f"output_{'self0' if k < NH else 'mem0'}", k % NH) for k in (2 * n, 2 * n + 1)] for n in range(CT_D)})
            ffn(0)
            down_product(0, "h1")

            def pooled(k0, number, u_chunk):
                def run():
                    wait_taken(pe, u_chunk)
                    wait_taken(pe, u_chunk - 1)
                    pe.wait_ge(bands_ready, 2 * NG)
                    for ct in range(k0, k0 + number):
                        b, g = bank_for("pool", ct), ct // KG
                        pe.matmul(b[:, 0:T], u1[:, 0, ct * P:(ct + 1) * P], bandA[:, g, :], start=True, stop=False)
                        pe.matmul(b[:, P:T], u1[:, 1, ct * P:(ct + 1) * P], bandC[:, g, :], start=False, stop=True).then_inc(job_done, 1)
                return run

            def grouped(g):
                def run():
                    pe.wait_ge(wg_in, 16 * NG)
                    for ct in range(KG * g, KG * (g + 1)):
                        wait_emptied(pe, "pool", ct)
                    for dt in range(KG):
                        b = bank_for("group", KG * g + dt)
                        for ct in range(KG):
                            ins = pe.matmul(b[:, 0:T], wg[:, g, ct, dt * P:(dt + 1) * P], yT[:, KG * g + ct, :],
                                            start=(ct == 0), stop=(ct == KG - 1))
                        ins.then_inc(job_done, 1)
                return run

            def memory_queries():
                wait_taken(pe, CHUNK["in1"])
                transposes("qmem1", u1[:, :, PW:D], 0, MH)

            c = CHUNK["in1"]
            chunk(c, h_hi, h_lo, {1: new_input("h1", X_CHUNKS["down0"], 3)}, k_jobs("h1", range(CT_D)))
            chunk(c + 1, h_hi, h_lo, {3: memory_queries})
            wait_taken(pe, CHUNK["mem1"] + 1)
            chunk(c + 2, h_hi, h_lo, {s + 1: lambda s=s: attend("mem1", s) for s in range(MEM_STEPS)})
            chunk(c + 3, h_hi, h_lo, {2: pooled(0, 2 * KPC, c + 2), 5: grouped(0), 6: grouped(1)})
            out_product(1, {1: pooled(2 * KPC, KPC, c + 3), 2: grouped(2), 3: grouped(3)},
                        {n: [("group", k) if k < NH else ("output_mem1", k - NH) for k in (2 * n, 2 * n + 1)] for n in range(CT_D)})
            ffn(1)
            down_product(1, None)


INPUTS = ["x", "mem", "mixer_norm", "ffn_norm", "final_norm", "mem_norm", "w_mem_kv", "w_out", "w_gate", "w_up", "w_down",
          "w_in_attn", "q_norm", "kv_norm", "w_uq", "w_uk", "w_uv", "w_idx_uq", "idx_k_norm", "idx_k_bias",
          "w_in_pool", "w_pool_group", "pool_scale"]


def kernel(**inputs):
    import numpy as np
    import concourse.bacc as bacc
    from concourse.bass_utils import run_bass_kernel_spmd

    nc = bacc.Bacc("TRN2", target_bir_lowering=False, num_devices=1)
    arrays, args = {}, []
    for name in INPUTS:
        a = np.ascontiguousarray(inputs[name])
        arrays[f"in_{name}"] = a
        args.append(nc.dram_tensor(f"in_{name}", a.shape, mybir.dt.from_np(a.dtype), kind="ExternalInput").ap())
    y = nc.dram_tensor("y", arrays["in_x"].shape, F32, kind="ExternalOutput").ap()
    trunk(nc, *args, y)
    result = run_bass_kernel_spmd(nc, [arrays], core_ids=[0])
    return result.results[0]["y"]
```
